# Optimizing a Trainium2 kernel written in Bass

```python
import jax, jax.numpy as jnp
from jax import lax
import numpy as np

D_MODEL = 1024
BATCH = 1
SEQ = 512
DEPTH = 1

CHUNK = 64
MIX_WIDTH = D_MODEL
SGU_WIDTH = MIX_WIDTH // 2
SGU_HEADS = 8
SGU_HEAD_DIM = SGU_WIDTH // SGU_HEADS
SGU_BLOCK = 128
RWKV_WIDTH = MIX_WIDTH - SGU_WIDTH
RWKV_HEAD_DIM = 64
RWKV_HEADS = RWKV_WIDTH // RWKV_HEAD_DIM
DECAY_LORA = 64
ICLR_LORA = 64
GATE_LORA = 128
LNX_EPS = 64e-5
IN_WIDTH = 2 * SGU_WIDTH + 3 * RWKV_WIDTH
N_EXPERTS = 32
TOP_K = 4
D_EXPERT = D_MODEL
SWIGLU_ALPHA = 1.702
SWIGLU_LIMIT = 7.0
MOE_BLOCK = 128
RMS_EPS = 1e-5
LN_EPS = 1e-5

kernel_name = "hymba_sgu_rwkv7_moe_block"

def rms_norm(x, g):
    xf = x.astype(jnp.float32)
    y = xf * lax.rsqrt(jnp.mean(xf * xf, axis=-1, keepdims=True) + RMS_EPS)
    return (y * g.astype(jnp.float32)).astype(x.dtype)

def token_shift(z):
    return jnp.pad(z, ((0, 0), (1, 0), (0, 0)))[:, :-1]

def shift_mix(z, mu):
    return z + (token_shift(z) - z) * mu

def chunk_causal_mask(n):
    c = jnp.arange(n) // CHUNK
    return c[None, :] <= c[:, None]

def spatial_gating(z, ln_g, ln_b, w_s, b_s):
    b, s, _ = z.shape
    u, v = jnp.split(z, 2, axis=-1)
    vf = v.astype(jnp.float32)
    mu = jnp.mean(vf, axis=-1, keepdims=True)
    var = jnp.mean(jnp.square(vf - mu), axis=-1, keepdims=True)
    v = ((vf - mu) * lax.rsqrt(var + LN_EPS) * ln_g.astype(jnp.float32)
         + ln_b.astype(jnp.float32)).astype(z.dtype)
    v = v.reshape(b, s // SGU_BLOCK, SGU_BLOCK, SGU_HEADS, SGU_HEAD_DIM)
    w = jnp.where(chunk_causal_mask(SGU_BLOCK)[None], w_s, jnp.zeros_like(w_s))
    sv = jnp.einsum('hij,bnjhc->bnihc', w, v) + jnp.transpose(b_s)[None, None, :, :, None]
    return u * sv.reshape(b, s, SGU_WIDTH).astype(u.dtype)

def rwkv7_time_mix(hn, p_r, p_k, p_v, mu_rkv, mu_wag, w0, w1, w2, a0, a1, a2,
                   g1, g2, k_k, k_a, r_k, lnx_g, lnx_b):
    f32 = jnp.float32
    b, s, _ = hn.shape
    H, N = RWKV_HEADS, RWKV_HEAD_DIM
    hd = (b, s, H, N)
    r = shift_mix(p_r, mu_rkv[0]).astype(f32).reshape(hd)
    k = shift_mix(p_k, mu_rkv[1]).astype(f32).reshape(hd)
    v = shift_mix(p_v, mu_rkv[2]).astype(f32).reshape(hd)
    xw = shift_mix(hn, mu_wag[0])
    xa = shift_mix(hn, mu_wag[1])
    xg = shift_mix(hn, mu_wag[2])
    w = -jax.nn.softplus(-(w0 + jnp.tanh(xw @ w1) @ w2).astype(f32)) - 0.5
    decay = jnp.exp(-jnp.exp(w)).reshape(hd)
    iclr = jax.nn.sigmoid((a0 + (xa @ a1) @ a2).astype(f32)).reshape(hd)
    gate = (jax.nn.sigmoid(xg @ g1) @ g2).astype(f32)
    kk = k * k_k.astype(f32).reshape(H, N)
    kk = kk / jnp.maximum(jnp.sqrt(jnp.sum(kk * kk, axis=-1, keepdims=True)), 1e-12)
    k = k * (1.0 + (iclr - 1.0) * k_a.astype(f32).reshape(H, N))

    def step(state, inp):
        r_t, w_t, k_t, v_t, a_t, b_t = inp
        sa = jnp.einsum('bhvk,bhk->bhv', state, a_t)
        state = (state * w_t[:, :, None, :] + sa[..., None] * b_t[:, :, None, :]
                 + v_t[..., None] * k_t[:, :, None, :])
        return state, jnp.einsum('bhvk,bhk->bhv', state, r_t)

    seq_first = lambda z: jnp.moveaxis(z, 1, 0)
    xs = (seq_first(r), seq_first(decay), seq_first(k), seq_first(v),
          seq_first(-kk), seq_first(kk * iclr))
    state0 = jnp.zeros((b, H, N, N), f32)
    _, y = lax.scan(step, state0, xs)
    y = jnp.moveaxis(y, 0, 1)
    mu = jnp.mean(y, axis=-1, keepdims=True)
    var = jnp.mean(jnp.square(y - mu), axis=-1, keepdims=True)
    y = ((y - mu) * lax.rsqrt(var + LNX_EPS) * lnx_g.astype(f32).reshape(H, N)
         + lnx_b.astype(f32).reshape(H, N))
    y = y + jnp.sum(r * k * r_k.astype(f32), axis=-1, keepdims=True) * v
    return (y.reshape(b, s, RWKV_WIDTH) * gate).astype(hn.dtype)

def clamped_swiglu(hid):
    x_glu, x_lin = hid[..., ::2], hid[..., 1::2]
    x_glu = jnp.minimum(x_glu, SWIGLU_LIMIT)
    x_lin = jnp.clip(x_lin, -SWIGLU_LIMIT, SWIGLU_LIMIT)
    return x_glu * jax.nn.sigmoid(SWIGLU_ALPHA * x_glu) * (x_lin + 1.0)

def moe_ffn(h, router_w, router_b, w1, b1, w2, b2):
    b, s, d = h.shape
    t = b * s
    hf = h.reshape(t, d)
    logits = (hf @ router_w + router_b).astype(jnp.float32)
    top_val, top_idx = lax.top_k(logits, TOP_K)
    gates = jax.nn.softmax(top_val, axis=-1)
    n_assign = t * TOP_K
    e_flat = top_idx.reshape(-1).astype(jnp.int32)
    tok_flat = (jnp.arange(n_assign, dtype=jnp.int32) // TOP_K)
    gate_flat = gates.reshape(-1)
    order = jnp.argsort(e_flat)
    e_sorted = e_flat[order]
    counts = jnp.bincount(e_flat, length=N_EXPERTS).astype(jnp.int32)
    padded = (counts + MOE_BLOCK - 1) // MOE_BLOCK * MOE_BLOCK
    start = jnp.cumsum(counts) - counts
    pad_end = jnp.cumsum(padded)
    pad_start = pad_end - padded
    dest = pad_start[e_sorted] + jnp.arange(n_assign, dtype=jnp.int32) - start[e_sorted]
    n_blocks = -(-n_assign // MOE_BLOCK) + N_EXPERTS
    n_rows = n_blocks * MOE_BLOCK
    row_tok = jnp.full((n_rows,), t, jnp.int32).at[dest].set(tok_flat[order])
    row_gate = jnp.zeros((n_rows,), jnp.float32).at[dest].set(gate_flat[order])
    block_start = jnp.arange(n_blocks, dtype=jnp.int32) * MOE_BLOCK
    block_expert = jnp.minimum(jnp.searchsorted(pad_end, block_start, side='right'),
                               N_EXPERTS - 1).astype(jnp.int32)
    hpad = jnp.concatenate([hf, jnp.zeros((1, d), hf.dtype)], axis=0)
    xin = hpad[row_tok].reshape(n_blocks, MOE_BLOCK, d)

    def expert_block(args):
        xb, e = args
        hid = xb @ w1[e] + b1[e]
        return clamped_swiglu(hid) @ w2[e] + b2[e]

    yout = lax.map(expert_block, (xin, block_expert)).reshape(n_rows, d)
    y = jnp.zeros((t + 1, d), jnp.float32).at[row_tok].add(
        yout.astype(jnp.float32) * row_gate[:, None])
    return y[:t].reshape(b, s, d).astype(h.dtype)

def setup_inputs(seed: int = 0) -> dict:
    key = jax.random.key(seed)
    ks = iter(jax.random.split(key, 40))
    L, D = DEPTH, D_MODEL
    nrm = lambda shape, scale: jax.random.normal(next(ks), shape, jnp.float32) * scale
    gain = lambda shape: 1.0 + nrm(shape, 0.05)
    uni = lambda shape, lo, hi: jax.random.uniform(next(ks), shape, jnp.float32, lo, hi)
    return {
        "x": nrm((BATCH, SEQ, D), 1.0),
        "norm1_g": gain((L, D)),
        "w_in": nrm((L, D, IN_WIDTH), D ** -0.5),
        "sgu_ln_g": gain((L, SGU_WIDTH)),
        "sgu_ln_b": nrm((L, SGU_WIDTH), 0.05),
        "sgu_w": nrm((L, SGU_HEADS, SGU_BLOCK, SGU_BLOCK), SGU_BLOCK ** -0.5),
        "sgu_b": 1.0 + nrm((L, SGU_HEADS, SGU_BLOCK), 0.1),
        "mu_rkv": uni((L, 3, RWKV_WIDTH), 0.0, 1.0),
        "mu_wag": uni((L, 3, D), 0.0, 1.0),
        "decay_w0": uni((L, RWKV_WIDTH), -5.5, 1.0),
        "decay_w1": nrm((L, D, DECAY_LORA), D ** -0.5),
        "decay_w2": nrm((L, DECAY_LORA, RWKV_WIDTH), 0.5 * DECAY_LORA ** -0.5),
        "iclr_a0": nrm((L, RWKV_WIDTH), 0.1),
        "iclr_a1": nrm((L, D, ICLR_LORA), D ** -0.5),
        "iclr_a2": nrm((L, ICLR_LORA, RWKV_WIDTH), ICLR_LORA ** -0.5),
        "gate_g1": nrm((L, D, GATE_LORA), D ** -0.5),
        "gate_g2": nrm((L, GATE_LORA, RWKV_WIDTH), GATE_LORA ** -0.5),
        "k_k": 0.85 + nrm((L, RWKV_WIDTH), 0.05),
        "k_a": gain((L, RWKV_WIDTH)),
        "r_k": nrm((L, RWKV_HEADS, RWKV_HEAD_DIM), 0.1),
        "lnx_g": gain((L, RWKV_WIDTH)),
        "lnx_b": nrm((L, RWKV_WIDTH), 0.05),
        "w_out": nrm((L, MIX_WIDTH, D), MIX_WIDTH ** -0.5),
        "norm2_g": gain((L, D)),
        "router_w": nrm((L, D, N_EXPERTS), D ** -0.5),
        "router_b": nrm((L, N_EXPERTS), 0.01),
        "moe_w1": nrm((L, N_EXPERTS, D, 2 * D_EXPERT), D ** -0.5),
        "moe_b1": nrm((L, N_EXPERTS, 2 * D_EXPERT), 0.01),
        "moe_w2": nrm((L, N_EXPERTS, D_EXPERT, D), D_EXPERT ** -0.5),
        "moe_b2": nrm((L, N_EXPERTS, D), 0.01),
        "final_g": gain((D,)),
    }

def reference(x, norm1_g, w_in, sgu_ln_g, sgu_ln_b, sgu_w, sgu_b, mu_rkv, mu_wag,
              decay_w0, decay_w1, decay_w2, iclr_a0, iclr_a1, iclr_a2, gate_g1, gate_g2,
              k_k, k_a, r_k, lnx_g, lnx_b, w_out, norm2_g, router_w, router_b,
              moe_w1, moe_b1, moe_w2, moe_b2, final_g):
    split_at = [2 * SGU_WIDTH, 2 * SGU_WIDTH + RWKV_WIDTH, 2 * SGU_WIDTH + 2 * RWKV_WIDTH]
    h = x
    for l in range(DEPTH):
        hn = rms_norm(h, norm1_g[l])
        proj = hn @ w_in[l]
        z_a, p_r, p_k, p_v = jnp.split(proj, split_at, axis=-1)
        y_a = spatial_gating(jax.nn.gelu(z_a, approximate=False),
                             sgu_ln_g[l], sgu_ln_b[l], sgu_w[l], sgu_b[l])
        y_b = rwkv7_time_mix(hn, p_r, p_k, p_v, mu_rkv[l], mu_wag[l],
                             decay_w0[l], decay_w1[l], decay_w2[l],
                             iclr_a0[l], iclr_a1[l], iclr_a2[l], gate_g1[l], gate_g2[l],
                             k_k[l], k_a[l], r_k[l], lnx_g[l], lnx_b[l])
        h = h + jnp.concatenate([y_a, y_b], axis=-1) @ w_out[l]
        h = h + moe_ffn(rms_norm(h, norm2_g[l]), router_w[l], router_b[l],
                        moe_w1[l], moe_b1[l], moe_w2[l], moe_b2[l])
    return rms_norm(h, final_g)


_drawn_inputs = setup_inputs


def setup_inputs(seed=0):
    import zlib

    import numpy as np

    out = dict(_drawn_inputs(seed))
    spreads = {}
    factors = {'moe_b1': 8.0, 'moe_b2': 8.0}
    for name, (base, spread) in spreads.items():
        noise = np.random.default_rng([zlib.crc32(name.encode()), seed]).standard_normal(out[name].shape)
        drawn = base * np.exp(spread * noise) if base else spread * noise
        out[name] = __import__('jax').numpy.asarray(drawn.astype(out[name].dtype))
    for name, factor in factors.items():
        out[name] = (out[name] * factor).astype(out[name].dtype)
    return out
```

```python
from contextlib import ExitStack

import numpy as np

import concourse.bass as bass
from concourse import mybir

ACT = mybir.ActivationFunctionType
ALU = mybir.AluOpType
AX_X = mybir.AxisListType.X
F32 = mybir.dt.float32
F32R = mybir.dt.float32r
I32 = mybir.dt.int32
U32 = mybir.dt.uint32

P = 128
D = 1024
T = 512
NT = T // P
KD = D // P
SG = 512
NF = SG // P
H = 8
HD = 64
C = P
LEVELS = 6
E = 32
TOPK = 4
NOVF = (T * TOPK) // (P + 1)
NB = E + NOVF
NT1 = NB + 1
FE = 2 * D
LIMIT = 7.0
ALPHA = 1.702
DECAY = float(np.exp(-0.5))
RMS_EPS = 1e-5
LN_EPS = 1e-5
LNX_EPS = 64e-5


def columns(*named):
    at, out = 0, {}
    for name, width in named:
        out[name] = slice(at, at + width)
        at += width
    return out, at


CST, NCST = columns(("ident", P), ("tri", 2 * C), ("mask", 4 * C), ("below", P), ("lev1", P),
                    ("ones", P), ("ident64", HD), ("head", NF * H), ("iota_e", E), ("iota_b", NT1),
                    ("iota_r", P), ("tok", NT), ("half", H * NT), ("over", E + 1), ("part", 1))
VEC, NVEC = columns(("norm1", KD), ("mu_rkv", 3 * NF), ("mu_wag", 3 * KD), ("a0", NF),
                    ("k_k", NF), ("k_a", NF), ("r_k", NF))


def constants():
    c = np.zeros((P, NCST), np.float32)
    s, t = np.arange(P)[:, None], np.arange(P)[None, :]
    c[:, CST["ident"]] = s == t
    mid = (s < C // 2).astype(np.float32)
    c[:, CST["tri"]] = -DECAY * np.concatenate([(s <= t) - mid, (s < t) - mid], 1)
    c[:, CST["mask"]] = np.concatenate([s < t, s <= t, s < t, s <= t], 1)
    c[:, CST["below"]] = s < t
    c[:, CST["lev1"]] = (s % 2 == 0) & (t == s + 1)
    c[:, CST["ones"]] = 1
    c[:, CST["ident64"]] = (s % HD) == np.arange(HD)[None, :]
    head = np.zeros((P, NF, H), np.float32)
    for f in range(NF):
        for q in range(2):
            head[HD * q:HD * q + HD, f, 2 * f + q] = 1
    c[:, CST["head"]] = head.reshape(P, -1)
    c[:, CST["iota_e"]] = np.arange(E)
    c[:, CST["iota_b"]] = np.arange(NT1)
    c[:, CST["iota_r"]] = np.arange(P)
    c[:, CST["tok"]] = np.arange(NT)[None, :] * P + s
    c[:, CST["half"]] = -0.5
    c[:E, CST["over"]] = np.concatenate([np.arange(E)[:, None] < np.arange(E)[None, :], np.ones((E, 1))], 1)
    c[:, CST["part"]] = s % E
    lev = np.zeros((P, LEVELS, HD), np.int32)
    for l in range(LEVELS):
        b = 2 << l
        col = np.arange(HD)
        lev[:, l, :] = (s // b) == (2 * (col // b) + 1)[None, :]
    return c, lev.reshape(P, -1)


class Chain:

    def __init__(self, eng, sem, base=0):
        self.eng, self.sem, self.base, self.n = eng, sem, base, 0

    def __call__(self, ins):
        ins.then_inc(self.sem, 1)
        self.n += 1
        self.eng.wait_ge(self.sem, self.base + self.n)


def program(nc, a):
    with ExitStack() as whole:
        sems = {}

        def sem(name):
            if name not in sems:
                sems[name] = whole.enter_context(nc.semaphore(name))
            return sems[name]

        def sb(stack, name, shape, dt=F32):
            return stack.enter_context(nc.sbuf_tensor(name, shape, dt))

        PS = whole.enter_context(nc.psum_tensor("PS", [P, 8, 512], F32))
        ring = sb(whole, "ring", [P, 12, FE])
        cst = sb(whole, "cst", [P, NCST])
        tok_of_row = sb(whole, "tok_of_row", [P, NT1], I32)
        slot_of = sb(whole, "slot_of", [P, NT * TOPK], I32)
        gate_of = sb(whole, "gate_of", [P, NT * TOPK])
        sel_of_block = sb(whole, "sel_of_block", [2 * E, NT1])
        expert_of_block = sb(whole, "expert_of_block", [1, NT1], I32)
        n_blocks = sb(whole, "n_blocks", [1, 2], I32)
        ident = cst[:, CST["ident"]]

        xn_dram = nc.dram_tensor("xn_rows", [T, D], F32, kind="Internal").ap()
        h_dram = nc.dram_tensor("h_rows", [T, D], F32, kind="Internal").ap()
        y_dram = nc.dram_tensor("y_rows", [NB * P, D], F32, kind="Internal").ap()
        w1_rows = a["moe_w1"].rearrange("l e (k p) f -> l e k p f", p=P)
        w2_rows = a["moe_w2"].rearrange("l e (k p) f -> l e p k f", p=P)

        with ExitStack() as st:
            first_half(nc, st, a, sem, sb, PS, ring, cst, tok_of_row, slot_of, gate_of,
                       sel_of_block, expert_of_block, n_blocks, xn_dram, h_dram, y_dram, w1_rows)
        with ExitStack() as st:
            experts(nc, st, a, sem, sb, PS, ring, cst, tok_of_row, slot_of, gate_of,
                    sel_of_block, expert_of_block, n_blocks, xn_dram, h_dram, y_dram, w1_rows, w2_rows)


def first_half(nc, st, a, sem, sb, PS, ring, cst, tok_of_row, slot_of, gate_of,
               sel_of_block, expert_of_block, n_blocks, xn_dram, h_dram, y_dram, w1_rows):
    ident = cst[:, CST["ident"]]
    ones = cst[:, CST["ones"]]
    vec = sb(st, "vec", [P, NVEC])

    def v(name, n=None, i=0):
        s = VEC[name]
        return vec[:, s] if n is None else vec[:, s.start + n * i:s.start + n * i + n]

    flat = ring[:, :, :].rearrange("p a b -> p (a b)")
    w_rkv = flat[:, 0:KD * 1536].rearrange("p (k n) -> p k n", k=KD)
    w_uv = flat[:, KD * 1536:KD * 2560].rearrange("p (k n) -> p k n", k=KD)
    w_out = flat[:, KD * 1536:KD * 1536 + KD * D].rearrange("p (k n) -> p k n", k=KD)
    lora_w = flat[:, 20480:22528].rearrange("p (k n) -> p k n", k=KD)
    lora_s = flat[:, 22528:24576].rearrange("p (k n) -> p k n", k=KD)

    def lent(at, *dims):
        n = int(np.prod(dims))
        names = "abcd"[:len(dims)]
        view = flat[:, at:at + n]
        if len(dims) > 1:
            view = view.rearrange(f"p ({' '.join(names)}) -> p {' '.join(names)}",
                                  **dict(zip(names, dims)))
        return view, at + n

    at = 0
    am, at = lent(at, H, 4 * C)
    sgt, at = lent(at, SG)
    ar, at = lent(at, NF, 2, C)
    loopb, at = lent(at, 12, SG)
    assert at <= KD * 1536
    at = KD * 1536
    wsT, at = lent(at, H, C)
    ln_rows, at = lent(at, 2, SG)
    bs, at = lent(at, NF * C)
    at = 20480
    uT, at = lent(at, NF, T)
    vN, at = lent(at, NF, SG)
    at = 20480
    anv, at = lent(at, H, 2 * HD)
    pq, at = lent(at, H, 2 * HD)
    tb, at = lent(at, H, C)
    ub, at = lent(at, H, C)
    assert at <= 24576

    x_t = sb(st, "x_t", [P, 2, D])
    hnT = sb(st, "hnT", [P, KD, T + 1])
    yT = hnT[:, :, 0:T]
    pT = [sb(st, f"p{n}T", [P, NF, T + 1]) for n in "rkv"]
    rT, kT, vT = pT
    dT = sb(st, "dT", [P, 2, T])
    icT = sb(st, "icT", [P, NF, T])
    kkT = sb(st, "kkT", [P, NF, T])
    sgN = sb(st, "sgN", [P, NT, SG])
    gateT = sb(st, "gateT", [P, T])
    tw = sb(st, "tw", [HD + 1, T])
    ia = sb(st, "ia", [P, T])
    lora_w2 = sb(st, "lora_w2", [HD + 1, SG])
    lora_a2 = sb(st, "lora_a2", [P, SG])
    lora_g2 = sb(st, "lora_g2", [P, SG])
    lev = sb(st, "lev", [P, LEVELS * HD], I32)
    small = sb(st, "small", [P, 256])
    headrk = sb(st, "headrk", [P, NF * H])
    rows = sb(st, "rows", [P, 2, SG])
    (e_in, e_ex, e_inv, b_t, k_t, rk_t, bN, kN, vNt, z_b, gT, y_b) = (loopb[:, i, :] for i in range(12))
    sT = sb(st, "sT", [P, NF * HD])
    s0 = sb(st, "s0", [P, NF * HD])
    fT = sb(st, "fT", [P, NF * HD])
    blank = sb(st, "blank", [P, 256])
    gsl = sb(st, "gsl", [P, P])
    v_sl = sb(st, "v_sl", [P, NF * C])
    y2 = dT[:, 0, :]
    y3 = dT[:, 1, :]
    ss = small[:, 0:NT]
    rstd = small[:, NT:2 * NT]
    bnst = small[:, 16:16 + 6]
    bnag = small[:, 24:24 + 2 * NT]
    vr = small[:, 32:32 + NT]
    omka = small[:, 40:40 + NF]
    kks = small[:, 48:48 + H * NT]
    kkr = small[:, 80:80 + H * NT]
    e_m = small[:, 112:112 + NF]
    mean = small[:, 120:128]
    var = small[:, 128:136]
    rs = small[:, 136:144]

    x_rows = a["x"].rearrange("b (j p) d -> (b j) p d", p=P)
    w_in = a["w_in"].rearrange("l (k p) n -> (l p) k n", p=P)
    w_out_d = a["w_out"].rearrange("l (k p) n -> (l p) k n", p=P)
    N_ACT_USES = 30

    def hN(j):
        return kkT[:, :, :].rearrange("p a b -> p (a b)")[:, (j % 2) * D:(j % 2 + 1) * D] if j < 2 else \
            icT[:, :, :].rearrange("p a b -> p (a b)")[:, (j % 2) * D:(j % 2 + 1) * D]

    def xN(j):
        return sgN[:, :, :].rearrange("p a b -> p (a b)")[:, (j % 2) * D:(j % 2 + 1) * D] if j < 2 else \
            rT[:, :, :].rearrange("p a b -> p (a b)")[:, (j % 2) * D:(j % 2 + 1) * D]

    norm2 = kT[:, :, :].rearrange("p a b -> p (a b)")[:, 0:D]
    router_w = vT[:, :, :].rearrange("p a b -> p (a b)")[:, 0:KD * E].rearrange("p (k e) -> p k e", k=KD)
    router_b = vT[:, :, :].rearrange("p a b -> p (a b)")[:, 256:256 + E]
    xnT = vT[:, :, :].rearrange("p a b -> p (a b)")[:, 512:512 + D].rearrange("p (k t) -> p k t", k=KD)
    route = hnT[:, :, :].rearrange("p a b -> p (a b)")
    roh = x_t[:, :, :].rearrange("p a b -> p (a b)").rearrange("p (i r) -> p i r", i=16)
    r_at = {}
    at = 0
    for name, n in (("logit", NT * E), ("top", NT * 8), ("idxf", NT * TOPK), ("oh", NT * TOPK * E),
                    ("m", NT * E), ("rank", NT * E), ("cntT", 8), ("ovfB", P), ("ovs", E + 1),
                    ("tmp", NT * TOPK * E), ("rk", 16), ("q", 16), ("q2", 16), ("blk", 16), ("ov", 16),
                    ("e0", 16), ("boh", 16 * NT1), ("ex", 16), ("sm", 4), ("sr", 4)):
        r_at[name] = route[:, at:at + n]
        at += n
    assert at <= KD * (T + 1)
    idxu = gateT[:, 0:NT * 8].bitcast(U32)

    AB_BANKS = (0, 1, 6, 7)

    def xs_view(j):
        return kkT[:, :, :].rearrange("p a b -> p (a b)")[:, (j % 2) * D:(j % 2 + 1) * D]

    def sq_view(n):
        return x_t[:, :, :].rearrange("p a b -> p (a b)")[:, n * SG:(n + 1) * SG]

    kkr_wide = sq_view

    exw = kT[:, :, :].rearrange("p a b -> p (a b)")[:, D:D + 16 * 2 * E].rearrange("p (i c) -> p i c", i=16)

    def xsq():
        return sgN[:, 0:2, :].rearrange("p a b -> p (a b)")

    def xsq2():
        return dT[:, :, :].rearrange("p a b -> p (a b)")

    block = st.enter_context(nc.Block())

    def f(n):
        return n.rearrange("p (f c) -> p f c", f=NF)

    @block.sync
    def _(sp):
        sp.dma_start(cst[:, :], a["cst"]).then_inc(sem("cst_in"), 16)
        for j in range(2):
            sp.dma_start(x_t[:, j, :], x_rows[j]).then_inc(sem(f"x_in{j}"), 16)
        sp.dma_start(vec[:, :], a["vec"]).then_inc(sem("vec_in"), 16)
        sp.dma_start(lora_w, a["lora_1"].rearrange("(k p) n -> p k n", p=P)).then_inc(sem("lora_in"), 16)
        sp.dma_start(lora_w2[:, :], a["lora_w2"]).then_inc(sem("lora2_in"), 16)
        sp.dma_start(lora_a2[HD:P, :], a["iclr_a2"][0]).then_inc(sem("lora2_in"), 16)
        sp.dma_start(lora_g2[:, :], a["gate_g2"][0]).then_inc(sem("lora2_in"), 16)
        for j in range(2, NT):
            sp.wait_ge(sem("xs_done"), j - 1)
            sp.dma_start(x_t[:, j % 2, :], x_rows[j]).then_inc(sem(f"x_in{j % 2}"), 16)
        for k in range(KD):
            sp.dma_start(w_uv[:, k, :], w_in[:, k, 0:2 * SG]).then_inc(sem("w_uv_in"), 16)
        for k in range(KD):
            sp.dma_start(w_rkv[:, k, :], w_in[:, k, 2 * SG:5 * SG]).then_inc(sem("w_rkv_in"), 16)
        sp.dma_start(lev[:, :], a["lev"]).then_inc(sem("lev_in"), 16)
        for i, name in enumerate(("lnx_g", "lnx_b")):
            sp.dma_start(rows[:, i, :], a[name].broadcast_to([P, SG])).then_inc(sem("lnx_in"), 16)
        sp.wait_ge(sem("filled"), 10 + 2 * NF)
        sp.dma_start(wsT, a["sgu_wT"]).then_inc(sem("ws_in"), 16)
        for i, name in enumerate(("sgu_ln_g", "sgu_ln_b")):
            sp.dma_start(ln_rows[:, i, :], a[name].broadcast_to([P, SG])).then_inc(sem("rows_in"), 16)
        for q in range(2):
            src = a["sgu_b"][0].rearrange("(f q) i -> q f i", q=2)[q].rearrange("(o f) i -> o f i", o=1)
            sp.dma_start(f(bs)[HD * q:HD * q + HD], src.broadcast_to([HD, NF, C])).then_inc(sem("bs_in"), 16)
        sp.wait_ge(sem("sgu_out"), NF)
        sp.dma_start(w_out, w_out_d).then_inc(sem("w_out_in"), 16)
        sp.wait_ge(sem("zeros"), 7)
        for b in range(E, NB):
            sp.dma_start(y_dram[b * P:(b + 1) * P, :].rearrange("p (a c) -> p a c", c=256),
                         blank[:, :].rearrange("p (o c) -> p o c", o=1).broadcast_to([P, D // 256, 256])).then_inc(sem("blanked"), 16)
        for j in range(2):
            sp.wait_ge(sem("kk_turned"), NF)
            sp.dma_start(x_t[:, j, :], x_rows[j]).then_inc(sem(f"x_in{j}"), 16)
        sp.wait_ge(sem("pe_tile"), NT + 1)
        sp.wait_ge(sem("act_tile"), NT + 1)
        sp.wait_ge(sem("dve_tile"), NT + 1)
        for k in range(6):
            sp.dma_start(ring[:, k, :], w1_rows[0, 0, k]).then_inc(sem(f"w_in{k}"), 16)
        for j in range(2, NT):
            sp.wait_ge(sem("h_done"), j - 1)
            sp.dma_start(x_t[:, j % 2, :], x_rows[j]).then_inc(sem(f"x_in{j % 2}"), 16)
        sp.wait_ge(sem("out_proj"), NT)
        for k in range(6, KD):
            sp.dma_start(ring[:, k, :], w1_rows[0, 0, k]).then_inc(sem(f"w_in{k}"), 16)
        for j in range(NT):
            sp.wait_ge(sem("xn_done"), j + 1)
            sp.dma_start(h_dram[j * P:(j + 1) * P, :], hN(j)).then_inc(sem("rows_out"), 16)
            sp.dma_start(xn_dram[j * P:(j + 1) * P, :], xN(j)).then_inc(sem("rows_out"), 16)
        sp.wait_ge(sem("rows_out"), 16 * 2 * NT)
        sp.wait_ge(sem("blanked"), 16 * NOVF)

    @block.gpsimd
    def _(pool):
        zeros = Chain(pool, sem("zeros"))
        zeros(nc.gpsimd.memset(hnT[:, :, 0:1], 0.0))
        for p_ in pT:
            zeros(nc.gpsimd.memset(p_[:, :, 0:1], 0.0))
        zeros(nc.gpsimd.memset(tw[HD:HD + 1, :], 1.0))
        zeros(nc.gpsimd.memset(sT[:, :], 0.0))
        zeros(nc.gpsimd.memset(blank[:, :], 0.0))
        pool.wait_ge(sem("cst_in"), 16)
        half = cst[:, CST["half"]]
        for j in range(NT):
            pool.wait_ge(sem("ms1"), j + 1)
            nc.gpsimd.tensor_tensor(rstd[:, j:j + 1], ss[:, j:j + 1], half[:, 0:1], ALU.pow).then_inc(sem("rstd1"), 1)
            pool.wait_ge(sem("rstd1"), j + 1)
        pool.wait_ge(sem("ws_in"), 16)
        nc.gpsimd.memset(wsT[HD:P, :, 0:HD], 0.0).then_inc(sem("ws_masked"), 1)
        pool.wait_ge(sem("ws_masked"), 1)
        pool.wait_ge(sem("ln_var"), 1)
        nc.gpsimd.tensor_tensor(vr, vr, half[:, 0:NT], ALU.pow).then_inc(sem("ln_rs"), 1)
        pool.wait_ge(sem("ln_rs"), 1)
        pool.wait_ge(sem("kk_ss"), 1)
        nc.gpsimd.tensor_tensor(kkr, kks, half, ALU.pow).then_inc(sem("kk_rs"), 1)
        pool.wait_ge(sem("kk_rs"), 1)
        with pool.Fori(0, NT) as j:
            pool.wait_ge(sem("pe_tile"), j + 1)
            pool.sem_inc(sem("wait_only_pool"), 1)
            nc.gpsimd.tensor_copy(sgt, sgN[:, bass.ds(j, 1), :].rearrange("p a b -> p (a b)")).then_inc(sem("sliced"), 1)
            pool.wait_ge(sem("sliced"), j * 3 + 1)
            pool.sem_inc(sem("wait_only_pool"), 1)
            nc.gpsimd.tensor_copy(f(v_sl[:, :]), vT[:, :, bass.ds(j * C + 1, C)]).then_inc(sem("sliced"), 1)
            pool.wait_ge(sem("sliced"), j * 3 + 2)
            pool.sem_inc(sem("wait_only_pool"), 1)
            nc.gpsimd.tensor_copy(gsl[:, :], gateT[:, bass.ds(j * C, C)]).then_inc(sem("sliced"), 1)
            pool.wait_ge(sem("sliced"), j * 3 + 3)
            pool.wait_ge(sem("lnx_var"), j + 1)
            nc.gpsimd.tensor_tensor(rs, var, half[:, 0:H], ALU.pow).then_inc(sem("lnx_rs"), 1)
            pool.wait_ge(sem("lnx_rs"), j + 1)
        for j in range(NT):
            pool.wait_ge(sem("ms2"), j + 1)
            nc.gpsimd.tensor_tensor(rstd[:, j:j + 1], ss[:, j:j + 1], half[:, 0:1], ALU.pow).then_inc(sem("rstd2"), 1)
            pool.wait_ge(sem("rstd2"), j + 1)

    @block.tensor
    def _(pe):
        pe.wait_ge(sem("cst_in"), 16)
        for j in range(NT):
            pe.wait_ge(sem("xs_done"), j + 1)
            for k in range(KD):
                m = nc.tensor.transpose(PS[:, 2 * j + k // 4, (k % 4) * P:(k % 4 + 1) * P], xs_view(j)[:, k * P:(k + 1) * P], ident)
            m.then_inc(sem("xT"), 1)
        pe.wait_ge(sem("hn_done"), 2 * NT)
        pe.wait_ge(sem("zeros"), 7)
        use = [0]

        def bank():
            u = use[0]
            use[0] += 1
            if u >= 6:
                pe.wait_ge(sem("emptied"), u - 5)
            return PS[:, u % 6, :]

        now, before = slice(1, T + 1), slice(0, T)
        pe.wait_ge(sem("lora_mixed"), 2)
        for m_ in range(2):
            out = bank()
            for k in range(KD):
                pe.matmul(out, lora_w[:, k, m_ * P:(m_ + 1) * P], hnT[:, k, now], start=(k == 0), stop=False)
                m = pe.matmul(out, lora_s[:, k, m_ * P:(m_ + 1) * P], hnT[:, k, before], start=False, stop=(k == KD - 1))
            m.then_inc(sem("filled"), 1)
        pe.wait_ge(sem("lora2_in"), 48)
        pe.wait_ge(sem("emptied"), 2)
        for n in range(NF):
            pe.matmul(bank(), lora_a2[HD:P, n * P:(n + 1) * P], ia[HD:P, :], start=True, stop=True).then_inc(sem("filled"), 1)
        for j in range(NT):
            pe.matmul(bank(), tw[:, j * P:(j + 1) * P], lora_w2[:, :], start=True, stop=True).then_inc(sem("filled"), 1)
        pe.wait_ge(sem("w_uv_in"), 16 * KD)
        for n in range(NF):
            out = bank()
            for k in range(KD):
                m = pe.matmul(out, w_uv[:, k, n * P:(n + 1) * P], hnT[:, k, now], start=(k == 0), stop=(k == KD - 1))
            m.then_inc(sem("filled"), 1)
        for j in range(NT):
            out = bank()
            for k in range(KD):
                m = pe.matmul(out, hnT[:, k, 1 + j * P:1 + (j + 1) * P], w_uv[:, k, SG:2 * SG],
                              start=(k == 0), stop=(k == KD - 1))
            m.then_inc(sem("filled"), 1)
        pe.wait_ge(sem("w_rkv_in"), 16 * KD)

        def project(i, n):
            out = bank()
            for k in range(KD):
                m = pe.matmul(out, w_rkv[:, k, i * SG + n * P:i * SG + (n + 1) * P], hnT[:, k, now],
                              start=(k == 0), stop=(k == KD - 1))
            m.then_inc(sem("filled"), 1)

        for n in range(NF):
            project(1, n)
        pe.wait_ge(sem("ws_masked"), 1)
        pe.wait_ge(sem("ln_done"), NT)
        for n in range(NF):
            if n >= 1:
                pe.wait_ge(sem("mix_read"), n)
            for q in range(2):
                for j in range(NT):
                    h = 2 * n + q
                    m = pe.matmul(PS[HD * q:HD * q + HD, 7, j * P:(j + 1) * P], vN[:, j, h * HD:(h + 1) * HD],
                                  wsT[:, h, :], start=True, stop=True, skip_group_check=True)
            m.then_inc(sem("sgu_mixed"), 1)
            project(0, n)
        pe.wait_ge(sem("kk_sq"), NF)
        for j in range(NT):
            for n in range(NF):
                m = pe.matmul(PS[:, 6, j * H:(j + 1) * H], sq_view(n)[:, j * P:(j + 1) * P],
                              cst[:, CST["head"]][:, n * H:(n + 1) * H], start=(n == 0), stop=(n == NF - 1))
        m.then_inc(sem("kk_len"), 1)
        for n in range(NF):
            project(2, n)
            pe.wait_ge(sem("kk_wide"), n + 1)
            if n >= 1:
                pe.wait_ge(sem("kk_scaled"), n)
            for j in range(NT):
                m = nc.tensor.transpose(PS[:, 6, j * P:(j + 1) * P], kkr_wide(n)[:, j * P:(j + 1) * P], ident)
            m.then_inc(sem("kk_turned"), 1)
        assert use[0] == N_ACT_USES

        with pe.Fori(0, NT) as j:
            pe.wait_ge(sem("act_tile"), j + 1)
            pe.wait_ge(sem("dve_tile"), j + 1)
            pe.wait_ge(sem("sliced"), j * 3 + 3)
            for n in range(NF):
                m = pe.matmul(PS[:, n // 2, (n % 2) * 2 * C:(n % 2 + 1) * 2 * C], sgt[:, n * P:(n + 1) * P],
                              cst[:, CST["tri"]], start=True, stop=True, skip_group_check=True)
            m.then_inc(sem("cw"), 1)

            def turn(src, b):
                for n in range(NF):
                    m = nc.tensor.transpose(PS[:, b, n * P:(n + 1) * P], src[:, n, :], ident)
                m.then_inc(sem("turned"), 1)

            turn(f(v_sl[:, :]), 5)
            pe.wait_ge(sem("prep"), j * 5 + 1)
            turn(ar[:, :, 0, :], 2)
            pe.wait_ge(sem("prep"), j * 5 + 3)
            turn(f(b_t), 3)
            pe.wait_ge(sem("prep"), j * 5 + 4)
            turn(f(k_t), 4)
            for h in range(H):
                n, p0 = h // 2, HD * (h % 2)
                b = AB_BANKS[h % 4]
                if h == 0:
                    pe.wait_ge(sem("exps"), j * 4 + 4)
                if h >= 4:
                    pe.wait_ge(sem("am_done"), j * H + h - 3)
                rhs = ar[p0:p0 + HD, n, :, :].rearrange("p a b -> p (a b)")
                pe.matmul(PS[:, b, 0:2 * C], f(b_t)[p0:p0 + HD, n, :], rhs, start=True, stop=True, skip_group_check=True)
                pe.matmul(PS[:, b, 2 * C:4 * C], f(k_t)[p0:p0 + HD, n, :], rhs, start=True, stop=True,
                          skip_group_check=True).then_inc(sem("ab"), 1)
            pe.wait_ge(sem("am_done"), j * H + H)
            pe.wait_ge(sem("turned_out"), j * 4 + 4)
            for h in range(H):
                m = pe.matmul(PS[:, 7, h * HD:(h + 1) * HD], am[:, h, 2 * C:3 * C], vNt[:, h * HD:(h + 1) * HD],
                              start=True, stop=True, skip_group_check=True)
            m.then_inc(sem("mv"), 1)
            for g in range(2):
                pe.wait_ge(sem("u_init"), j * 2 + g + 1)
                for h in range(4):
                    m = nc.tensor.transpose(PS[:, 4 + g, h * P:(h + 1) * P], ub[:, 4 * g + h, :], ident)
                m.then_inc(sem("t_turned"), 1)
            for l in range(LEVELS):
                b = 2 << l
                for g in range(2):
                    pe.wait_ge(sem("t_done"), j * 2 * (LEVELS + 1) + 2 * l + g + 1)
                    if l:
                        pe.wait_ge(sem("z_done"), j * 2 * LEVELS + 2 * l + g - 1)
                    for h in range(4):
                        even = tb[:, 4 * g + h, :].rearrange("p (n t b) -> p n t b", t=2, b=b)[:, :, 0, :]
                        m = pe.matmul(PS[:, 2 + g, h * HD:(h + 1) * HD], am[:, 4 * g + h, 0:C], even,
                                      start=True, stop=True, skip_group_check=True)
                    m.then_inc(sem("z"), 1)
                for g in range(2):
                    pe.wait_ge(sem("z_done"), j * 2 * LEVELS + 2 * l + g + 1)
                    if l:
                        pe.wait_ge(sem("u_done"), j * 2 * LEVELS + 2 * (l - 1) + g + 1)
                    for h in range(4):
                        m = pe.matmul(PS[:, 2 + g, 256 + h * HD:256 + (h + 1) * HD], ub[:, 4 * g + h, :],
                                      z_b[:, g * 256 + h * HD:g * 256 + (h + 1) * HD], start=True, stop=True,
                                      skip_group_check=True)
                    m.then_inc(sem("x"), 1)
                for g in range(2):
                    pe.wait_ge(sem("t_done"), j * 2 * (LEVELS + 1) + 2 * (l + 1) + g + 1)
                    for h in range(4):
                        m = nc.tensor.transpose(PS[:, 4 + g, h * P:(h + 1) * P], tb[:, 4 * g + h, :], ident)
                    m.then_inc(sem("u"), 1)
            pe.wait_ge(sem("mv_out"), j + 1)
            for h in range(H):
                if h % 4 == 0:
                    pe.wait_ge(sem("u_done"), j * 2 * LEVELS + 2 * (LEVELS - 1) + h // 4 + 1)
                m = pe.matmul(PS[:, h // 4, (h % 4) * C:(h % 4 + 1) * C], ub[:, h, :], anv[:, h, :],
                              start=True, stop=True, skip_group_check=True)
                if h % 4 == 3:
                    m.then_inc(sem("pq"), 1)
            pe.matmul(PS[:, 6, :], gsl[:, :], lora_g2[:, :], start=True, stop=True)
            pe.wait_ge(sem("prep"), j * 5 + 5)
            for n in range(NF):
                m = pe.matmul(PS[:, 7, 0:H], f(rk_t)[:, n, :], headrk[:, n * H:(n + 1) * H], start=(n == 0), stop=(n == NF - 1))
            m.then_inc(sem("bonus"), 1)
            for h in range(H):
                n, p0 = h // 2, HD * (h % 2)
                if h % 4 == 0:
                    pe.wait_ge(sem("pq_out"), j * 2 + h // 4 + 1)
                pe.matmul(PS[p0:p0 + HD, 2, n * C:(n + 1) * C], pq[:, h, 0:HD], am[:, h, C:2 * C],
                          start=True, stop=True, skip_group_check=True)
                m = pe.matmul(PS[p0:p0 + HD, 3, n * HD:(n + 1) * HD], pq[:, h, 0:HD], bN[:, h * HD:(h + 1) * HD],
                              start=True, stop=True, skip_group_check=True)
            m.then_inc(sem("gf"), 1)
            pe.wait_ge(sem("gf_out"), j * 2 + 2)
            for h in range(H):
                n, p0 = h // 2, HD * (h % 2)
                hv = slice(h * HD, (h + 1) * HD)
                st_ = PS[p0:p0 + HD, 4, n * HD:(n + 1) * HD]
                pe.matmul(st_, bN[:, hv], pq[:, h, HD:2 * HD], start=True, stop=False, skip_group_check=True)
                pe.matmul(st_, kN[:, hv], vNt[:, hv], start=False, stop=False, skip_group_check=True)
                m = pe.matmul(st_, fT[p0:p0 + HD, n * HD:(n + 1) * HD], s0[p0:p0 + HD, n * HD:(n + 1) * HD],
                              start=False, stop=True, skip_group_check=True)
            m.then_inc(sem("state"), 1)
            for h in range(H):
                n, p0 = h // 2, HD * (h % 2)
                hv = slice(h * HD, (h + 1) * HD)
                yo = PS[:, 1 + 4 * (h % 2), n * HD:(n + 1) * HD]
                pe.matmul(yo, am[:, h, C:2 * C], pq[:, h, HD:2 * HD], start=True, stop=False, skip_group_check=True)
                pe.matmul(yo, am[:, h, 3 * C:4 * C], vNt[:, hv], start=False, stop=False, skip_group_check=True)
                m = pe.matmul(yo, f(gT)[p0:p0 + HD, n, :], s0[p0:p0 + HD, n * HD:(n + 1) * HD],
                              start=False, stop=True, skip_group_check=True)
            m.then_inc(sem("y"), 1)
            pe.wait_ge(sem("dve_tile"), j + 2)
            for n in range(NF):
                m = nc.tensor.transpose(PS[:, 0, n * P:(n + 1) * P], y_b[:, n * P:(n + 1) * P], ident)
            m.then_inc(sem("pe_tile"), 1)

        pe.wait_ge(sem("w_out_in"), 16)
        pe.wait_ge(sem("act_tile"), NT + 1)
        pe.wait_ge(sem("sgu_out"), NF)
        for j in range(NT):
            b = 2 * (j % 2)
            if j >= 2:
                pe.wait_ge(sem("h_done"), j - 1)
            for n in range(2):
                for k in range(KD):
                    m = pe.matmul(PS[:, b + n, :], yT[:, k, j * P:(j + 1) * P], w_out[:, k, n * 512:(n + 1) * 512],
                                  start=(k == 0), stop=(k == KD - 1))
            m.then_inc(sem("out_proj"), 1)
        pe.wait_ge(sem("router_in"), 32)
        for j in range(NT):
            pe.wait_ge(sem("xn_done"), j + 1)
            if j:
                pe.wait_ge(sem("xnT_out"), j)
            for k in range(KD):
                m = nc.tensor.transpose(PS[:, 4 + k // 4, (k % 4) * P:(k % 4 + 1) * P], xN(j)[:, k * P:(k + 1) * P], ident)
            m.then_inc(sem("xn_turned"), 1)
            pe.wait_ge(sem("xnT_out"), j + 1)
            for k in range(KD):
                m = pe.matmul(PS[:, 6, j * E:(j + 1) * E], xnT[:, k, :], router_w[:, k, :],
                              start=(k == 0), stop=(k == KD - 1))
            m.then_inc(sem("logits"), 1)
        pe.wait_ge(sem("mask_m"), 1)
        mm = r_at["m"].rearrange("p (j e) -> p j e", j=NT)
        for j in range(NT):
            for i in range(j):
                pe.matmul(PS[:, 0, j * E:(j + 1) * E], ones, mm[:, i, :], start=(i == 0), stop=False)
            pe.matmul(PS[:, 0, j * E:(j + 1) * E], cst[:, CST["below"]], mm[:, j, :], start=(j == 0), stop=True)
        for j in range(NT):
            m = pe.matmul(PS[0:E, 1, 0:1], mm[:, j, :], ones[:, 0:1], start=(j == 0), stop=(j == NT - 1))
        m.then_inc(sem("counts"), 1)
        pe.wait_ge(sem("ovf_b"), 1)
        pe.matmul(PS[:, 2, 0:E + 1], r_at["ovfB"][0:E, :], cst[0:E, CST["over"]], start=True, stop=True).then_inc(sem("ovf_sum"), 1)
        pe.wait_ge(sem("onehots"), 1)
        boh = r_at["boh"].rearrange("p (i b) -> p i b", i=16)
        ex = r_at["ex"]
        for i in range(16):
            m = pe.matmul(PS[:, 3, 0:NT1], roh[:, i, :], boh[:, i, :], start=(i == 0), stop=(i == 15))
        m.then_inc(sem("tok_table"), 1)
        pe.wait_ge(sem("exw"), 1)
        for i in range(16):
            m = pe.matmul(PS[0:2 * E, 4, 0:NT1], exw[:, i, :], boh[:, i, :], start=(i == 0), stop=(i == 15))
        m.then_inc(sem("exp_table"), 1)

    @block.scalar
    def _(act):
        for j in range(NT):
            act.wait_ge(sem(f"x_in{j % 2}"), 16 * (j // 2 + 1))
            if j:
                act.wait_ge(sem("sumsq1"), j)
            nc.scalar.activation(xsq(), x_t[:, j % 2, :], ACT.Square, accum_out=ss[:, j:j + 1]).then_inc(sem("sumsq1"), 1)
        use = [0]

        def filled():
            act.wait_ge(sem("filled"), use[0] + 1)
            u = use[0]
            use[0] += 1
            return PS[:, u % 6, :]

        b = filled()
        nc.scalar.activation(tw[0:HD, :], b[0:HD, :], ACT.Tanh)
        nc.scalar.activation(ia[HD:P, :], b[HD:P, :], ACT.Copy).then_inc(sem("emptied"), 1)
        nc.scalar.activation(gateT[:, :], filled(), ACT.Sigmoid).then_inc(sem("emptied"), 1)
        for n in range(NF):
            nc.scalar.activation(icT[:, n, :], filled(), ACT.Sigmoid, bias=v("a0", 1, n)).then_inc(sem("emptied"), 1)
        for j in range(NT):
            nc.scalar.activation(sgN[:, j, :], filled(), ACT.Sigmoid).then_inc(sem("emptied"), 1)
        for n in range(NF):
            nc.scalar.activation(uT[:, n, :], filled(), ACT.Gelu).then_inc(sem("emptied"), 1)
        for j in range(NT):
            nc.scalar.activation(vN[:, j, :], filled(), ACT.Gelu).then_inc(sem("emptied"), 1)
        for i in (1, 0, 2):
            for n in range(NF):
                nc.scalar.activation(pT[i][:, n, 1:T + 1], filled(), ACT.Copy).then_inc(sem("emptied"), 1)
        act.wait_ge(sem("sgu_moved"), 1)
        act.sem_inc(sem("act_tile"), 1)
        with act.Fori(0, NT) as j:
            act.wait_ge(sem("cw"), j + 1)
            cw = PS[:, 0:2, :].rearrange("p a b -> p (a b)").rearrange("p (f c) -> p f c", f=NF)
            nc.scalar.activation(f(e_ex), cw[:, :, C:2 * C], ACT.Exp).then_inc(sem("exps"), 1)
            nc.scalar.activation(f(e_in), cw[:, :, 0:C], ACT.Exp).then_inc(sem("exps"), 1)
            nc.scalar.activation(f(e_inv), cw[:, :, 0:C], ACT.Exp, scale=-1.0).then_inc(sem("exps"), 1)
            nc.scalar.activation(e_m.rearrange("p (f o) -> p f o", o=1), cw[:, :, C:C + 1], ACT.Exp, scale=-1.0).then_inc(sem("exps"), 1)
            for i, (dst, b) in enumerate(((vNt, 5), (anv[:, :, 0:HD], 2), (bN, 3), (kN, 4))):
                act.wait_ge(sem("turned"), j * 4 + i + 1)
                src = PS[:, b, :]
                if i == 1:
                    src = src.rearrange("p (h d) -> p h d", h=H)
                nc.scalar.activation(dst, src, ACT.Copy).then_inc(sem("turned_out"), 1)
            act.wait_ge(sem("mv"), j + 1)
            nc.scalar.activation(anv[:, :, HD:2 * HD], PS[:, 7, :].rearrange("p (h d) -> p h d", h=H), ACT.Copy).then_inc(sem("mv_out"), 1)
            for l in range(LEVELS):
                for g in range(2):
                    act.wait_ge(sem("z"), j * 2 * LEVELS + 2 * l + g + 1)
                    nc.scalar.activation(z_b[:, g * 256:(g + 1) * 256], PS[:, 2 + g, 0:256], ACT.Copy).then_inc(sem("z_done"), 1)
                for g in range(2):
                    act.wait_ge(sem("u"), j * 2 * LEVELS + 2 * l + g + 1)
                    nc.scalar.activation(ub[:, 4 * g:4 * g + 4, :].rearrange("p h t -> p (h t)"), PS[:, 4 + g, :], ACT.Copy).then_inc(sem("u_done"), 1)
            for i in range(2):
                act.wait_ge(sem("pq"), j * 2 + i + 1)
                nc.scalar.activation(pq[:, 4 * i:4 * i + 4, :].rearrange("p h t -> p (h t)"), PS[:, i, :], ACT.Copy).then_inc(sem("pq_out"), 1)
            act.wait_ge(sem("pe_tile"), j + 2)
            nc.scalar.activation(yT[:, NF:2 * NF, bass.ds(j * C, C)], f(PS[:, 0, :]), ACT.Copy).then_inc(sem("act_tile"), 1)
        act.wait_ge(sem("pe_tile"), NT + 1)
        act.wait_ge(sem("dve_tile"), NT + 1)
        act.dma_start(norm2, a["norm2_g"].broadcast_to([P, D])).then_inc(sem("norm2_in"), 16)
        act.dma_start(router_w, a["router_w"].rearrange("l (k p) e -> (l p) k e", p=P)).then_inc(sem("router_in"), 16)
        act.dma_start(router_b, a["router_b"].broadcast_to([P, E])).then_inc(sem("router_in"), 16)
        for j in range(NT):
            act.wait_ge(sem("h_done"), j + 1)
            if j:
                act.wait_ge(sem("sumsq2"), j)
            nc.scalar.activation(xsq2(), hN(j), ACT.Square, accum_out=ss[:, j:j + 1]).then_inc(sem("sumsq2"), 1)
        act.wait_ge(sem("gate_in"), 1)
        top = r_at["top"].rearrange("p (j t) -> p j t", j=NT)
        nc.scalar.activation(gate_of[:, :].rearrange("p (j k) -> p j k", j=NT), top[:, :, 0:TOPK], ACT.Exp).then_inc(sem("gate_exp"), 1)

    @block.vector
    def _(dve):
        step = Chain(dve, sem("dve_step"))
        dve.wait_ge(sem("cst_in"), 16)
        dve.wait_ge(sem("vec_in"), 16)

        def scale(j):
            dve.wait_ge(sem("rstd1"), j + 1)
            if j >= 2:
                dve.wait_ge(sem("xT"), j - 1)
            nc.vector.tensor_scalar(xs_view(j), x_t[:, j % 2, :], rstd[:, j:j + 1], None, ALU.mult).then_inc(sem("xs_done"), 1)

        def evac(j):
            dve.wait_ge(sem("xT"), j + 1)
            for q in range(2):
                g = v("norm1")[:, 4 * q:4 * q + 4].rearrange("p (k o) -> p k o", o=1).broadcast_to([P, 4, P])
                nc.vector.tensor_tensor(hnT[:, 4 * q:4 * q + 4, 1 + j * P:1 + (j + 1) * P],
                                        PS[:, 2 * j + q, :].rearrange("p (k t) -> p k t", k=4), g, ALU.mult).then_inc(sem("hn_done"), 1)

        for j in range(NT):
            dve.wait_ge(sem("sumsq1"), j + 1)
            nc.vector.tensor_scalar(ss[:, j:j + 1], ss[:, j:j + 1], 1.0 / D, RMS_EPS, ALU.mult, ALU.add).then_inc(sem("ms1"), 1)
            scale(j)
            if j:
                evac(j - 1)
        dve.wait_ge(sem("lora_in"), 16)
        mw = v("mu_wag").rearrange("p (i k o) -> p i k o", i=3, o=1)
        for i, (lo, n) in enumerate(((0, HD), (HD, HD), (P, P))):
            step(nc.vector.tensor_tensor(lora_s[:, :, lo:lo + n], lora_w[:, :, lo:lo + n],
                                         mw[:, i].broadcast_to([P, KD, n]), ALU.mult))
        nc.vector.tensor_tensor(lora_w, lora_w, lora_s, ALU.subtract).then_inc(sem("lora_mixed"), 2)
        evac(NT - 1)
        nc.vector.tensor_scalar(omka, v("k_a"), -1.0, 1.0, ALU.mult, ALU.add).then_inc(sem("omka"), 1)
        for n in range(NF):
            step(nc.vector.tensor_scalar(headrk[:, n * H:(n + 1) * H], cst[:, CST["head"]][:, n * H:(n + 1) * H],
                                         v("r_k", 1, n), None, ALU.mult))

        def mix(i, n, at):
            dve.wait_ge(sem("emptied"), at + n + 1)
            step(nc.vector.tensor_tensor(dT[:, 0, :], pT[i][:, n, 0:T], pT[i][:, n, 1:T + 1], ALU.subtract))
            step(nc.vector.scalar_tensor_tensor(pT[i][:, n, 1:T + 1], dT[:, 0, :], v("mu_rkv", NF, i)[:, n:n + 1],
                                                pT[i][:, n, 1:T + 1], ALU.mult, ALU.add))

        dve.wait_ge(sem("rows_in"), 32)
        for j in range(NT):
            dve.wait_ge(sem("emptied"), 10 + NF + j + 1)
            step(nc.vector.bn_stats(bnst, vN[:, j, :]))
            step(nc.vector.bn_aggr(bnag[:, 2 * j:2 * j + 2], bnst))
        nc.vector.tensor_scalar(vr, bnag.rearrange("p (j t) -> p j t", t=2)[:, :, 1], LN_EPS, None, ALU.add).then_inc(sem("ln_var"), 1)
        dve.wait_ge(sem("ln_rs"), 1)
        for j in range(NT):
            step(nc.vector.tensor_scalar(vN[:, j, :], vN[:, j, :], bnag[:, 2 * j:2 * j + 1], vr[:, j:j + 1], ALU.subtract, ALU.mult))
            step(nc.vector.tensor_tensor(vN[:, j, :], vN[:, j, :], ln_rows[:, 0, :], ALU.mult))
            nc.vector.tensor_tensor(vN[:, j, :], vN[:, j, :], ln_rows[:, 1, :], ALU.add).then_inc(sem("ln_done"), 1)
        dve.wait_ge(sem("zeros"), 7)
        dve.wait_ge(sem("omka"), 1)
        for n in range(NF):
            mix(1, n, 18)
            step(nc.vector.tensor_scalar(kkT[:, n, :], kT[:, n, 1:T + 1], v("k_k", 1, n), None, ALU.mult))
            nc.vector.tensor_tensor(sq_view(n), kkT[:, n, :], kkT[:, n, :], ALU.mult).then_inc(sem("kk_sq"), 1)
            step(nc.vector.tensor_scalar(dT[:, 1, :], icT[:, n, :], v("k_a", 1, n), omka[:, n:n + 1], ALU.mult, ALU.add))
            step(nc.vector.tensor_tensor(kT[:, n, 1:T + 1], kT[:, n, 1:T + 1], dT[:, 1, :], ALU.mult))
        dve.wait_ge(sem("bs_in"), 32)
        for n in range(NF):
            dve.wait_ge(sem("sgu_mixed"), n + 1)
            b4 = f(bs)[:, n:n + 1, :].broadcast_to([P, NT, C])
            nc.vector.tensor_tensor(dT[:, 0, :].rearrange("p (j i) -> p j i", j=NT),
                                    PS[:, 7, :].rearrange("p (j i) -> p j i", j=NT), b4, ALU.add).then_inc(sem("mix_read"), 1)
            dve.wait_ge(sem("mix_read"), n + 1)
            nc.vector.tensor_tensor(uT[:, n, :], dT[:, 0, :], uT[:, n, :], ALU.mult).then_inc(sem("sgu_out"), 1)
            dve.wait_ge(sem("sgu_out"), n + 1)
            mix(0, n, 22)
        dve.wait_ge(sem("kk_len"), 1)
        nc.vector.tensor_scalar(kks, PS[:, 6, 0:H * NT], 1e-24, None, ALU.max).then_inc(sem("kk_ss"), 1)
        dve.wait_ge(sem("kk_rs"), 1)
        kkr4 = kkr.rearrange("p (j f q o) -> p j f q o", j=NT, f=NF, q=2)
        for n in range(NF):
            nc.vector.tensor_copy(kkr_wide(n).rearrange("p (j q c) -> p j q c", j=NT, q=2),
                                  kkr4[:, :, n].broadcast_to([P, NT, 2, HD])).then_inc(sem("kk_wide"), 1)
        for n in range(NF):
            mix(2, n, 26)
            dve.wait_ge(sem("kk_turned"), n + 1)
            nc.vector.tensor_tensor(kkT[:, n, :], kkT[:, n, :], PS[:, 6, :], ALU.mult).then_inc(sem("kk_scaled"), 1)
        dve.wait_ge(sem("filled"), N_ACT_USES)
        nc.vector.tensor_copy(yT[:, 0:NF, :], uT).then_inc(sem("sgu_moved"), 1)
        dve.wait_ge(sem("sgu_moved"), 1)
        dve.wait_ge(sem("sgu_out"), NF)
        dve.wait_ge(sem("lev_in"), 16)
        dve.wait_ge(sem("lnx_in"), 32)
        dve.sem_inc(sem("dve_tile"), 1)
        dve.sem_inc(sem("pe_tile"), 1)

        LOOP_STEPS = 16
        with dve.Fori(0, NT) as j:
            step = Chain(dve, sem("dve_chunk"), j * LOOP_STEPS)
            cols, cols1 = bass.ds(j * C, C), bass.ds(j * C + 1, C)
            dve.wait_ge(sem("act_tile"), j + 1)
            dve.wait_ge(sem("pe_tile"), j + 1)
            dve.wait_ge(sem("exps"), j * 4 + 1)
            nc.vector.scalar_tensor_tensor(ar[:, :, 0, :], kkT[:, :, cols], -1.0, f(e_ex), ALU.mult, ALU.mult).then_inc(sem("prep"), 1)
            dve.wait_ge(sem("exps"), j * 4 + 2)
            nc.vector.tensor_tensor(ar[:, :, 1, :], rT[:, :, cols1], f(e_in), ALU.mult).then_inc(sem("prep"), 1)
            step(nc.vector.tensor_tensor(f(b_t), kkT[:, :, cols], icT[:, :, cols], ALU.mult))
            dve.wait_ge(sem("exps"), j * 4 + 3)
            nc.vector.tensor_tensor(b_t, b_t, e_inv, ALU.mult).then_inc(sem("prep"), 1)
            nc.vector.tensor_tensor(f(k_t), kT[:, :, cols1], f(e_inv), ALU.mult).then_inc(sem("prep"), 1)
            nc.vector.tensor_tensor(f(rk_t), rT[:, :, cols1], kT[:, :, cols1], ALU.mult).then_inc(sem("prep"), 1)
            dve.wait_ge(sem("exps"), j * 4 + 4)
            step(nc.vector.tensor_tensor(f(s0[:, :]), f(sT[:, :]), e_m.rearrange("p (f o) -> p f o", o=1).broadcast_to([P, NF, HD]), ALU.mult))
            for h in range(H):
                dve.wait_ge(sem("ab"), j * H + h + 1)
                nc.vector.tensor_tensor(am[:, h, :], PS[:, AB_BANKS[h % 4], :], cst[:, CST["mask"]], ALU.mult).then_inc(sem("am_done"), 1)
                if h % 4 == 3:
                    g = h // 4
                    dve.wait_ge(sem("am_done"), j * H + h + 1)
                    u4 = ub[:, 4 * g:4 * g + 4, :]
                    l1 = cst[:, CST["lev1"]].rearrange("p (o t) -> p o t", o=1).broadcast_to([P, 4, C])
                    i1 = ident.rearrange("p (o t) -> p o t", o=1).broadcast_to([P, 4, C])
                    step(nc.vector.tensor_tensor(u4, am[:, 4 * g:4 * g + 4, 0:C], l1, ALU.mult))
                    nc.vector.tensor_tensor(u4, u4, i1, ALU.add).then_inc(sem("u_init"), 1)
            for g in range(2):
                dve.wait_ge(sem("t_turned"), j * 2 + g + 1)
                nc.vector.tensor_copy(tb[:, 4 * g:4 * g + 4, :].rearrange("p h t -> p (h t)"), PS[:, 4 + g, :]).then_inc(sem("t_done"), 1)
            for l in range(LEVELS):
                b = 2 << l
                for g in range(2):
                    dve.wait_ge(sem("x"), j * 2 * LEVELS + 2 * l + g + 1)
                    dve.sem_inc(sem("wait_only"), 1)
                    even = tb[:, 4 * g:4 * g + 4, :].rearrange("p h (n t b) -> p h n t b", t=2, b=b)[:, :, :, 0, :]
                    mask = lev[:, l * HD:(l + 1) * HD].rearrange("p (o n b) -> p o n b", o=1, b=b).broadcast_to([P, 4, HD // b, b])
                    xv = PS[:, 2 + g, 256:512].rearrange("p (h n b) -> p h n b", h=4, b=b)
                    nc.vector.copy_predicated(even, mask, xv).then_inc(sem("t_done"), 1)
            dve.wait_ge(sem("gf"), j + 1)
            i64 = cst[:, CST["ident64"]].rearrange("p (o t) -> p o t", o=1).broadcast_to([P, NF, HD])
            nc.vector.tensor_tensor(f(fT[:, :]), f(PS[:, 3, 0:NF * HD]), i64, ALU.add).then_inc(sem("gf_out"), 1)
            nc.vector.tensor_tensor(f(gT), f(PS[:, 2, :]), ar[:, :, 1, :], ALU.add).then_inc(sem("gf_out"), 1)
            dve.wait_ge(sem("state"), j + 1)
            step(nc.vector.tensor_tensor(f(sT[:, :]), f(PS[:, 4, 0:NF * HD]), f(e_in)[:, :, C - 1:C].broadcast_to([P, NF, HD]), ALU.mult))
            dve.wait_ge(sem("y"), j + 1)
            hd = lambda t: t.rearrange("p (h d) -> p h d", h=H)
            wide = lambda t: t.rearrange("p (h o) -> p h o", o=1).broadcast_to([P, H, HD])
            halves = lambda t, n: t.rearrange("p (n q d) -> p q n d", q=2, d=n)
            yP = PS[:, 1:6:4, 0:NF * HD].rearrange("p q (n d) -> p q n d", n=NF)
            step(nc.vector.tensor_reduce(halves(mean, 1), yP, AX_X, ALU.add))
            step(nc.vector.tensor_scalar(mean, mean, 1.0 / HD, None, ALU.mult))
            for q in range(2):
                step(nc.vector.tensor_tensor(halves(y_b, HD)[:, q], yP[:, q], halves(mean, 1)[:, q].broadcast_to([P, NF, HD]), ALU.subtract))
            step(nc.vector.tensor_tensor(y2, y_b, y_b, ALU.mult))
            step(nc.vector.tensor_reduce(var, hd(y2), AX_X, ALU.add))
            nc.vector.tensor_scalar(var, var, 1.0 / HD, LNX_EPS, ALU.mult, ALU.add).then_inc(sem("lnx_var"), 1)
            dve.wait_ge(sem("bonus"), j + 1)
            step(nc.vector.tensor_tensor(hd(y3), hd(vNt), PS[:, 7, 0:H].rearrange("p (h o) -> p h o", o=1).broadcast_to([P, H, HD]), ALU.mult))
            step(nc.vector.tensor_tensor(y3, y3, rows[:, 1, :], ALU.add))
            dve.wait_ge(sem("lnx_rs"), j + 1)
            step(nc.vector.tensor_tensor(hd(y_b), hd(y_b), wide(rs), ALU.mult))
            step(nc.vector.tensor_tensor(y_b, y_b, rows[:, 0, :], ALU.mult))
            step(nc.vector.tensor_tensor(y_b, y_b, y3, ALU.add))
            nc.vector.tensor_tensor(y_b, y_b, PS[:, 6, :], ALU.mult).then_inc(sem("dve_tile"), 1)
            assert step.n == LOOP_STEPS, step.n

        step = Chain(dve, sem("dve_step2"))
        dve.wait_ge(sem("pe_tile"), NT + 1)
        dve.wait_ge(sem("act_tile"), NT + 1)
        dve.wait_ge(sem("norm2_in"), 16)
        for j in range(NT):
            b = 2 * (j % 2)
            dve.wait_ge(sem("out_proj"), j + 1)
            dve.wait_ge(sem(f"x_in{j % 2}"), 16 * (j // 2 + 1 + 2))
            nc.vector.tensor_tensor(hN(j), PS[:, b:b + 2, :].rearrange("p a b -> p (a b)"), x_t[:, j % 2, :], ALU.add).then_inc(sem("h_done"), 1)
            dve.wait_ge(sem("sumsq2"), j + 1)
            nc.vector.tensor_scalar(ss[:, j:j + 1], ss[:, j:j + 1], 1.0 / D, RMS_EPS, ALU.mult, ALU.add).then_inc(sem("ms2"), 1)
            dve.wait_ge(sem("rstd2"), j + 1)
            nc.vector.scalar_tensor_tensor(xN(j), hN(j), rstd[:, j:j + 1], norm2, ALU.mult, ALU.mult).then_inc(sem("xn_done"), 1)
        for j in range(NT):
            dve.wait_ge(sem("xn_turned"), j + 1)
            if j:
                dve.wait_ge(sem("logits"), j)
            nc.vector.tensor_copy(xnT.rearrange("p k t -> p (k t)"), PS[:, 4:6, :].rearrange("p a b -> p (a b)")).then_inc(sem("xnT_out"), 1)
        jk = lambda t, n: t.rearrange("p (j e) -> p j e", j=NT)
        logit, top, idxf = jk(r_at["logit"], E), jk(r_at["top"], 8), r_at["idxf"]
        dve.wait_ge(sem("logits"), NT)
        dve.wait_ge(sem("router_in"), 32)
        step(nc.vector.tensor_tensor(logit, jk(PS[:, 6, 0:NT * E], E),
                                     router_b.rearrange("p (o e) -> p o e", o=1).broadcast_to([P, NT, E]), ALU.add))
        for j in range(NT):
            step(nc.vector.max(top[:, j, :], logit[:, j, :]))
            step(nc.vector.max_index(jk(idxu, 8)[:, j, :], top[:, j, :], logit[:, j, :]))
        step(nc.vector.tensor_copy(jk(idxf, TOPK), jk(idxu, 8)[:, :, 0:TOPK]))
        t4 = r_at["e0"]
        step(nc.vector.tensor_copy(t4[:, 0:NT].rearrange("p (j o) -> p j o", o=1), top[:, :, 0:1]))
        nc.vector.tensor_tensor(top[:, :, 0:TOPK], top[:, :, 0:TOPK],
                                t4[:, 0:NT].rearrange("p (j o) -> p j o", o=1).broadcast_to([P, NT, TOPK]), ALU.subtract).then_inc(sem("gate_in"), 1)
        oh = r_at["oh"].rearrange("p (i e) -> p i e", e=E)
        iota_e = cst[:, CST["iota_e"]].rearrange("p (o e) -> p o e", o=1).broadcast_to([P, 16, E])
        step(nc.vector.tensor_tensor(oh, idxf.rearrange("p (i o) -> p i o", o=1).broadcast_to([P, 16, E]), iota_e, ALU.is_equal))
        oh4 = r_at["oh"].rearrange("p (j k e) -> p j k e", j=NT, k=TOPK)
        m = jk(r_at["m"], E)
        step(nc.vector.tensor_tensor(m, oh4[:, :, 0], oh4[:, :, 1], ALU.add))
        step(nc.vector.tensor_tensor(m, m, oh4[:, :, 2], ALU.add))
        nc.vector.tensor_tensor(m, m, oh4[:, :, 3], ALU.add).then_inc(sem("mask_m"), 1)
        g16 = gate_of[:, :].rearrange("p (j k) -> p j k", j=NT)
        dve.wait_ge(sem("gate_exp"), 1)
        step(nc.vector.tensor_reduce(r_at["sm"], g16, AX_X, ALU.add))
        step(nc.vector.reciprocal(r_at["sr"], r_at["sm"]))
        step(nc.vector.tensor_tensor(g16, g16, r_at["sr"].rearrange("p (j o) -> p j o", o=1).broadcast_to([P, NT, TOPK]), ALU.mult))
        dve.wait_ge(sem("counts"), 1)
        cn = r_at["cntT"][0:E, :]
        step(nc.vector.tensor_copy(cn[:, 0:1], PS[0:E, 1, 0:1]))
        step(nc.vector.tensor_scalar(cn[:, 1:2], cn[:, 0:1], float(P), None, ALU.is_gt))
        for i in (2, 3):
            step(nc.vector.scalar_tensor_tensor(cn[:, i:i + 1], cn[:, 0:1], float(i * P), cn[:, i - 1:i], ALU.is_gt, ALU.add))
        nc.vector.tensor_scalar(r_at["ovfB"][0:E, :], ones[0:E, :], cn[:, 3:4], None, ALU.mult).then_inc(sem("ovf_b"), 1)
        rank = jk(r_at["rank"], E)
        step(nc.vector.tensor_copy(rank, jk(PS[:, 0, 0:NT * E], E)))
        tmp = r_at["tmp"].rearrange("p (j k e) -> p j k e", j=NT, k=TOPK)
        for kk_ in range(TOPK):
            step(nc.vector.tensor_tensor(tmp[:, :, kk_], oh4[:, :, kk_], rank, ALU.mult))
        rk, q, q2, blk, ov = (r_at[n] for n in ("rk", "q", "q2", "blk", "ov"))
        tmp16 = r_at["tmp"].rearrange("p (i e) -> p i e", e=E)
        step(nc.vector.tensor_reduce(rk, tmp16, AX_X, ALU.add))
        dve.wait_ge(sem("ovf_sum"), 1)
        ovs = r_at["ovs"]
        step(nc.vector.tensor_copy(ovs, PS[:, 2, 0:E + 1]))
        step(nc.vector.tensor_tensor(tmp16, oh, ovs[:, 0:E].rearrange("p (o e) -> p o e", o=1).broadcast_to([P, 16, E]), ALU.mult))
        step(nc.vector.tensor_reduce(ov, tmp16, AX_X, ALU.add))
        step(nc.vector.tensor_scalar(q, rk, float(P), None, ALU.is_ge))
        step(nc.vector.tensor_copy(q2, q))
        for i in (2, 3):
            step(nc.vector.scalar_tensor_tensor(q, rk, float(i * P), q, ALU.is_ge, ALU.add))
        step(nc.vector.scalar_tensor_tensor(rk, q, -float(P), rk, ALU.mult, ALU.add))
        step(nc.vector.tensor_tensor(blk, ov, q, ALU.add))
        step(nc.vector.scalar_tensor_tensor(blk, blk, float(E - 1), idxf, ALU.add, ALU.subtract))
        step(nc.vector.tensor_tensor(blk, blk, q2, ALU.mult))
        step(nc.vector.tensor_tensor(blk, blk, idxf, ALU.add))
        step(nc.vector.scalar_tensor_tensor(ov, blk, float(P), rk, ALU.mult, ALU.add))
        step(nc.vector.tensor_copy(slot_of[:, :], ov))
        boh = r_at["boh"].rearrange("p (i b) -> p i b", i=16)
        step(nc.vector.tensor_tensor(boh, blk.rearrange("p (i o) -> p i o", o=1).broadcast_to([P, 16, NT1]),
                                     cst[:, CST["iota_b"]].rearrange("p (o b) -> p o b", o=1).broadcast_to([P, 16, NT1]), ALU.is_equal))
        for i in range(16):
            s = cst[:, CST["tok"]]
            ins = nc.vector.tensor_scalar(roh[:, i, :], cst[:, CST["iota_r"]], rk[:, i:i + 1],
                                          s[:, i // TOPK:i // TOPK + 1], ALU.is_equal, ALU.mult)
            step(ins)
        dve.sem_inc(sem("onehots"), 1)
        step(nc.vector.scalar_tensor_tensor(r_at["ex"], rk, 0.0, idxf, ALU.is_equal, ALU.mult))
        step(nc.vector.tensor_copy(exw,
                                   r_at["ex"].rearrange("p (i o) -> p i o", o=1).broadcast_to([P, 16, 2 * E])))
        dve.sem_inc(sem("exw"), 1)
        dve.wait_ge(sem("tok_table"), 1)
        step(nc.vector.tensor_copy(tok_of_row[:, :], PS[:, 3, 0:NT1]))
        dve.wait_ge(sem("exp_table"), 1)
        et = route[:, 0:NT1]
        step(nc.vector.tensor_copy(et[:, 0:E], cst[:, CST["iota_b"]][:, 0:E]))
        step(nc.vector.tensor_copy(et[0:2 * E, E:NT1], PS[0:2 * E, 4, E:NT1]))
        step(nc.vector.tensor_copy(expert_of_block[:, :], et[0:1, :]))
        step(nc.vector.tensor_scalar(sel_of_block[:, :], et[0:2 * E, :], cst[0:2 * E, CST["part"]], None, ALU.is_equal))
        nb = small[0:1, 0:2]
        step(nc.vector.tensor_scalar(nb[:, 0:1], ovs[0:1, E:E + 1], float(E - 1), None, ALU.add))
        step(nc.vector.tensor_scalar(nb[:, 1:2], ovs[0:1, E:E + 1], float(E - 2), None, ALU.add))
        step(nc.vector.tensor_copy(n_blocks[:, :], nb))


def experts(nc, st, a, sem, sb, PS, ring, cst, tok_of_row, slot_of, gate_of,
            sel_of_block, expert_of_block, n_blocks, xn_dram, h_dram, y_dram, w1_rows, w2_rows):
    ident = cst[:, CST["ident"]]
    HL = 3
    CH = 12
    w_hi = sb(st, "w_hi", [P, HL, FE], F32R)
    w_lo = sb(st, "w_lo", [P, HL, FE], F32R)
    x_hi = sb(st, "x_hi", [P, D], F32R)
    x_lo = sb(st, "x_lo", [P, D], F32R)
    a_hi = sb(st, "a_hi", [P, D], F32R)
    a_lo = sb(st, "a_lo", [P, D], F32R)
    bias = sb(st, "bias", [2 * E, FE + D], F32R)
    pick_up = sb(st, "pick_up", [2 * E, P], F32R)
    pick_down = sb(st, "pick_down", [2 * E, P], F32R)
    x_rows = sb(st, "x_rows", [P, D])
    glu = sb(st, "glu", [P, D])
    sig = sb(st, "sig", [P, D])
    hid = sb(st, "hid", [P, D])
    y_out = sb(st, "y_out", [P, D])
    index = sb(st, "index", [P, 1], I32)
    idx4 = sb(st, "idx4", [P, 4], I32)
    stat = sb(st, "stat", [P, 16])
    flat = ring[:, :, :].rearrange("p a b -> p (a b)")
    bias_raw = flat[0:2 * E, 8 * FE:8 * FE + FE + D]
    h_rows = [flat[:, j * D:(j + 1) * D] for j in range(NT)]
    final_g = flat[:, NT * D:(NT + 1) * D]
    hidP = PS[:, 0:4, :].rearrange("p a b -> p (a b)")
    turnP = PS[:, 4:6, :].rearrange("p a b -> p (a b)")
    outP = PS[:, 6:8, :].rearrange("p a b -> p (a b)")
    picked_rows = (x_rows, glu, sig, hid)

    def one(i):
        return slice(i, i + 1) if isinstance(i, int) else bass.ds(i, 1)

    block = st.enter_context(nc.Block())

    def load_count(eng, less=0):
        return eng.value_load(n_blocks[0:1, less:less + 1], min_val=E - 1 - less, max_val=NB - 1 - less)

    @block.sync
    def _(sp):
        for q in range(2):
            sp.dma_start(bias_raw[q * E:(q + 1) * E, 0:FE], a["moe_b1"][0]).then_inc(sem("bias_in"), 16)
            sp.dma_start(bias_raw[q * E:(q + 1) * E, FE:FE + D], a["moe_b2"][0]).then_inc(sem("bias_in"), 16)
        n1 = load_count(sp)

        def expert(i):
            return sp.value_load(expert_of_block[0:1, one(i)], min_val=0, max_val=E - 1)

        def load_w2(e, before):
            for c in range(KD, CH):
                sp.wait_ge(sem("split"), before * CH + c + 1)
                k = 2 * (c - KD)
                sp.dma_start(ring[:, c, :].rearrange("p (k f) -> p k f", k=2),
                             w2_rows[0, one(e), :, k:k + 2, :].rearrange("o p k f -> (o p) k f")).then_inc(sem(f"w_in{c}"), 16)

        with sp.Fori(0, n1) as i0:
            i, before = i0 + 1, i0
            e1 = expert(i)
            for c in range(KD):
                sp.wait_ge(sem("split"), before * CH + c + 1)
                sp.dma_start(ring[:, c, :], w1_rows[0, one(e1), c].rearrange("o p f -> (o p) f")).then_inc(sem(f"w_in{c}"), 16)
            load_w2(expert(i0), i0)
        load_w2(expert(n1), n1)
        sp.wait_ge(sem("split"), n1 * CH + KD)
        for j in range(NT):
            sp.dma_start(h_rows[j], h_dram[j * P:(j + 1) * P, :]).then_inc(sem("h_in"), 16)
        sp.dma_start(final_g, a["final_g"].rearrange("(o d) -> o d", o=1).broadcast_to([P, D])).then_inc(sem("h_in"), 16)
        for j in range(NT):
            sp.wait_ge(sem("out_done"), j + 1)
            sp.dma_start(a["out"][0, j * P:(j + 1) * P, :], h_rows[j]).then_inc(sem("out_stored"), 16)
        sp.wait_ge(sem("out_stored"), 16 * NT)

    @block.gpsimd
    def _(pool):
        n1, n2 = load_count(pool), load_count(pool, 1)
        pool.sem_inc(sem("y_free"), 1)

        def gather(i):
            pool.sem_inc(sem("wait_only_pool"), 1)
            nc.gpsimd.tensor_copy(index[:, :], tok_of_row[:, one(i)]).then_inc(sem("index"), 1)
            pool.wait_ge(sem("index"), i + 1)
            pool.sem_inc(sem("wait_only_pool"), 1)
            nc.gpsimd.indirect_dma_start(x_rows[:, :], None, xn_dram,
                                         bass.IndirectOffsetOnAxis(index[:, :], 0)).then_inc(sem("x_rows_in"), 16)

        def gate(i):
            pool.wait_ge(sem("hid_read"), i + 1)
            nc.gpsimd.tensor_tensor(hid[:, :], hid[:, :], glu[:, :], ALU.mult).then_inc(sem("scaled"), 1)
            pool.wait_ge(sem("scaled"), i + 1)
            pool.wait_ge(sem("sig"), i + 1)
            nc.gpsimd.tensor_tensor(hid[:, :], hid[:, :], sig[:, :], ALU.mult).then_inc(sem("hid_done"), 1)
            pool.wait_ge(sem("hid_done"), i + 1)

        def store(i):
            pool.wait_ge(sem("y_ready"), i + 2)
            pool.dma_start(y_dram[bass.ds(i * P, P), :], y_out[:, :]).then_inc(sem("y_stored"), 16)
            pool.wait_ge(sem("y_stored"), (i + 1) * 16)
            pool.sem_inc(sem("y_free"), 1)

        gather(0)
        pool.wait_ge(sem("x_turned"), 1)
        gather(1)
        gate(0)
        pool.wait_ge(sem("x_turned"), 2)
        gather(2)
        gate(1)
        with pool.Fori(0, n2) as i1:
            i = i1 + 2
            store(i1)
            pool.wait_ge(sem("x_turned"), i + 1)
            gather(i + 1)
            gate(i)
        store(n2)
        store(n1)
        for j in range(NT + 1):
            for k in range(TOPK if j < NT else 0):
                q = j * TOPK + k
                if q >= 4:
                    pool.wait_ge(sem("summed"), q - 3)
                idx = idx4[:, q % 4:q % 4 + 1]
                nc.gpsimd.tensor_copy(idx, slot_of[:, q:q + 1]).then_inc(sem("index4"), 1)
                pool.wait_ge(sem("index4"), q + 1)
                nc.gpsimd.indirect_dma_start(picked_rows[q % 4][:, :], None, y_dram,
                                             bass.IndirectOffsetOnAxis(idx, 0)).then_inc(sem(f"row_in{q % 4}"), 16)
            if j:
                pool.wait_ge(sem("final_ms"), j)
                nc.gpsimd.tensor_tensor(stat[:, 7 + j:8 + j], stat[:, j - 1:j], cst[:, CST["half"]][:, 0:1], ALU.pow).then_inc(sem("final_rs"), 1)
                pool.wait_ge(sem("final_rs"), j)

    @block.tensor
    def _(pe):
        n1 = load_count(pe)

        def turn(src, done):
            for k in range(KD):
                m = nc.tensor.transpose(turnP[:, k * P:(k + 1) * P], src[:, k * P:(k + 1) * P], ident)
            m.then_inc(sem(done), 1)

        def turn_x(i):
            pe.wait_ge(sem("x_rows_in"), (i + 1) * 16)
            turn(x_rows, "x_turned")

        def turn_a(i):
            pe.wait_ge(sem("hid_done"), i + 1)
            pe.wait_ge(sem("x_split"), i + 2)
            turn(hid, "a_turned")

        def bias_rows(out, pick, lo, n_):
            for q in range(n_):
                pe.matmul(out[:, q * 512:(q + 1) * 512], pick[:, :], bias[:, lo + q * 512:lo + (q + 1) * 512],
                          start=True, stop=False, skip_group_check=True)

        def products(out, hi, lo, wh, wl, n_, stop):
            for x, w in ((hi, wh), (hi, wl), (lo, wh)):
                for q in range(n_):
                    m = pe.matmul(out[:, q * 512:(q + 1) * 512], x, w[:, q * 512:(q + 1) * 512], start=False,
                                  stop=stop and x is lo, skip_group_check=True)
            return m

        def up(i):
            first = isinstance(i, int)
            pe.wait_ge(sem("x_split"), i + 1)
            if not first:
                pe.wait_ge(sem("hid_read"), i)
            bias_rows(hidP, pick_up, 0, 4)
            for c in range(KD):
                pe.wait_ge(sem("split"), i * CH + c + 1)
                s = c % HL
                k = slice(c * P, (c + 1) * P)
                m = products(hidP, x_hi[:, k], x_lo[:, k], w_hi[:, s, :], w_lo[:, s, :], 4, c == KD - 1)
                m.then_inc(sem("used"), 5 if first and c == KD - 1 else 1)
                if c == 3 and not first:
                    turn_a(i0)

        def down(i, last=False):
            pe.wait_ge(sem("a_split"), i + 1)
            pe.wait_ge(sem("y_ready"), i + 1)
            bias_rows(outP, pick_down, FE, 2)
            for c in range(KD, CH):
                pe.wait_ge(sem("split"), (i + 1) * CH + (c - KD if last else c) + 1)
                s = (c - KD if last else c) % HL
                for kk in range(2):
                    k = 2 * (c - KD) + kk
                    ks, fs = slice(k * P, (k + 1) * P), slice(kk * D, (kk + 1) * D)
                    m = products(outP, a_hi[:, ks], a_lo[:, ks], w_hi[:, s, fs], w_lo[:, s, fs], 2, k == KD - 1)
                m.then_inc(sem("used"), 1)

        turn_x(0)
        up(0)
        turn_x(1)
        with pe.Fori(0, n1) as i0:
            i = i0 + 1
            up(i)
            pe.wait_ge(sem("a_split"), i)
            turn_x(i + 1)
            down(i0)
        turn_a(n1)
        down(n1, last=True)

    @block.scalar
    def _(act):
        act.wait_ge(sem("bias_in"), 64)
        act.wait_ge(sem("bias_one"), 1)
        nc.scalar.activation(bias[:, :], bias_raw, ACT.Copy).then_inc(sem("bias_hi"), 1)
        n1, n2 = load_count(act), load_count(act, 1)
        act.sem_inc(sem("y_ready"), 1)

        def high(c, i, last=False):
            cc = c - KD if last else c
            if not (isinstance(i, int) and i == 0 and c < HL):
                act.wait_ge(sem("used"), i * CH + (cc - HL + 1))
            act.wait_ge(sem(f"w_in{c}"), (i + 1) * 16 if c < KD else i * 16)
            first_end = isinstance(i, int) and i == 0 and c == KD - 1
            nc.scalar.activation(w_hi[:, cc % HL, :], ring[:, c, :], ACT.Copy).then_inc(sem("high"), 5 if first_end else 1)

        def x_high(i):
            act.wait_ge(sem("x_turned"), i + 1)
            nc.scalar.activation(x_hi[:, :], turnP, ACT.Copy).then_inc(sem("x_high"), 1)

        def a_high(i):
            act.wait_ge(sem("a_turned"), i + 1)
            nc.scalar.activation(a_hi[:, :], turnP, ACT.Copy).then_inc(sem("a_high"), 1)

        def sigmoid(i):
            act.wait_ge(sem("glu"), i + 1)
            nc.scalar.activation(sig[:, :], glu[:, :], ACT.Sigmoid, scale=ALPHA).then_inc(sem("sig"), 1)

        def out_rows(i, used):
            act.wait_ge(sem("used"), used)
            act.wait_ge(sem("y_free"), i + 1)
            nc.scalar.activation(y_out[:, :], outP, ACT.Copy).then_inc(sem("y_ready"), 1)

        x_high(0)
        for c in range(KD):
            high(c, 0)
        x_high(1)

        def step(i, i_1):
            high(0, i)
            sigmoid(i_1)
            high(1, i)
            if not isinstance(i, int):
                out_rows(i1, i1 * CH + 2 * CH)
            for c in range(2, 7):
                high(c, i)
            a_high(i_1)
            for c in range(7, 11):
                high(c, i)
            x_high(i + 1)
            high(11, i)

        step(1, 0)
        with act.Fori(0, n2) as i1:
            step(i1 + 2, i1 + 1)
        sigmoid(n1)
        out_rows(n2, n2 * CH + 2 * CH)
        a_high(n1)
        for c in range(KD, CH):
            high(c, n1 + 1, last=True)
        out_rows(n1, n1 * CH + CH + 4)
        for j in range(NT):
            act.wait_ge(sem("summed"), TOPK * (j + 1))
            if j:
                act.wait_ge(sem("final_sq"), j)
            nc.scalar.activation(y_out[:, :], h_rows[j], ACT.Square, accum_out=stat[:, j:j + 1]).then_inc(sem("final_sq"), 1)

    @block.vector
    def _(dve):
        linear = bias_raw[:, 0:FE].rearrange("p (f t) -> p f t", t=2)[:, :, 1]
        dve.wait_ge(sem("bias_in"), 64)
        nc.vector.tensor_scalar(linear, linear, 1.0, None, ALU.add).then_inc(sem("bias_one"), 1)
        dve.wait_ge(sem("bias_hi"), 1)
        low_half = slice(E, 2 * E)
        dve.wait_ge(sem("bias_one"), 1)
        nc.vector.tensor_tensor(bias[low_half, :], bias_raw[low_half, :], bias[low_half, :].bitcast(F32), ALU.subtract).then_inc(sem("bias_lo"), 1)
        n1 = load_count(dve)
        ones = cst[0:2 * E, CST["ones"]]

        def pick(dst, i):
            nc.vector.tensor_scalar(dst[:, :], ones, sel_of_block[:, one(i)], None, ALU.mult)

        def low(c, i, last=False):
            cc = c - KD if last else c
            dve.wait_ge(sem("high"), i * CH + cc + 1)
            s = cc % HL
            first_end = isinstance(i, int) and c == KD - 1
            nc.vector.tensor_tensor(w_lo[:, s, :], ring[:, c, :], w_hi[:, s, :].bitcast(F32), ALU.subtract) \
                .then_inc(sem("split"), 5 if first_end else 1)

        def x_low(i):
            dve.wait_ge(sem("x_high"), i + 1)
            pick(pick_up, i)
            nc.vector.tensor_tensor(x_lo[:, :], turnP, x_hi[:, :].bitcast(F32), ALU.subtract).then_inc(sem("x_split"), 1)

        def a_low(i):
            dve.wait_ge(sem("a_high"), i + 1)
            pick(pick_down, i)
            nc.vector.tensor_tensor(a_lo[:, :], turnP, a_hi[:, :].bitcast(F32), ALU.subtract).then_inc(sem("a_split"), 1)

        pairs = hidP.rearrange("p (f t) -> p f t", t=2)

        def clamp(i):
            dve.wait_ge(sem("used"), i * CH + KD)
            nc.vector.tensor_scalar(glu[:, :], pairs[:, :, 0], LIMIT, None, ALU.min).then_inc(sem("glu"), 1)
            nc.vector.tensor_scalar(hid[:, :], pairs[:, :, 1], LIMIT + 1, 1 - LIMIT, ALU.min, ALU.max).then_inc(sem("hid_read"), 1)

        x_low(0)
        for c in range(KD):
            low(c, 0)
        x_low(1)
        clamp(0)
        with dve.Fori(0, n1) as i0:
            i = i0 + 1
            for c in range(7):
                low(c, i)
            a_low(i0)
            for c in range(7, 11):
                low(c, i)
            x_low(i + 1)
            low(11, i)
            clamp(i)
        a_low(n1)
        for c in range(KD, CH):
            low(c, n1 + 1, last=True)
        dve.wait_ge(sem("h_in"), 16 * (NT + 1))
        for j in range(NT):
            for k in range(TOPK):
                q = j * TOPK + k
                dve.wait_ge(sem(f"row_in{q % 4}"), 16 * (q // 4 + 1))
                if k:
                    dve.wait_ge(sem("summed"), q)
                nc.vector.scalar_tensor_tensor(h_rows[j], picked_rows[q % 4][:, :], gate_of[:, q:q + 1], h_rows[j],
                                               ALU.mult, ALU.add).then_inc(sem("summed"), 1)
            dve.wait_ge(sem("final_sq"), j + 1)
            nc.vector.tensor_scalar(stat[:, j:j + 1], stat[:, j:j + 1], 1.0 / D, RMS_EPS, ALU.mult, ALU.add).then_inc(sem("final_ms"), 1)
            dve.wait_ge(sem("final_rs"), j + 1)
            nc.vector.scalar_tensor_tensor(h_rows[j], h_rows[j], stat[:, 8 + j:9 + j], final_g, ALU.mult, ALU.mult).then_inc(sem("out_done"), 1)


def features(x):
    return np.ascontiguousarray(x.reshape(-1, P).T)


def kernel(**inputs):
    import concourse.bacc as bacc
    from concourse.bass_utils import run_bass_kernel_spmd

    i = {k: np.asarray(v) for k, v in inputs.items()}
    cst, lev = constants()
    arrays = {n: i[n] for n in ("x", "w_in", "sgu_ln_g", "sgu_ln_b", "sgu_b", "iclr_a2", "gate_g2", "lnx_g", "lnx_b",
                                "w_out", "norm2_g", "router_w", "router_b", "moe_w1", "moe_b1", "moe_w2", "moe_b2",
                                "final_g")}
    arrays["cst"], arrays["lev"] = cst, lev
    arrays["vec"] = np.concatenate([features(i["norm1_g"][0])] + [features(i["mu_rkv"][0, q]) for q in range(3)]
                                   + [features(i["mu_wag"][0, q]) for q in range(3)]
                                   + [features(i[n][0]) for n in ("iclr_a0", "k_k", "k_a", "r_k")], 1)
    arrays["lora_1"] = np.concatenate([i["decay_w1"][0], i["iclr_a1"][0], i["gate_g1"][0]], 1)
    arrays["lora_w2"] = np.concatenate([i["decay_w2"][0], i["decay_w0"]], 0)
    arrays["sgu_wT"] = np.ascontiguousarray(i["sgu_w"][0].transpose(2, 0, 1))
    nc = bacc.Bacc("TRN2", target_bir_lowering=False, num_devices=1)
    a = {n: nc.dram_tensor("in_" + n, v.shape, mybir.dt.from_np(v.dtype), kind="ExternalInput").ap() for n, v in arrays.items()}
    a["out"] = nc.dram_tensor("out_rows", [1, T, D], F32, kind="ExternalOutput").ap()
    program(nc, a)
    r = run_bass_kernel_spmd(nc, [{"in_" + n: v for n, v in arrays.items()}], core_ids=[0])
    return r.results[0]["out_rows"]
```

```python
from contextlib import ExitStack

import numpy as np

import concourse.bass as bass
from concourse import mybir

ACT = mybir.ActivationFunctionType
ALU = mybir.AluOpType
AX_X = mybir.AxisListType.X
F32 = mybir.dt.float32
F32R = mybir.dt.float32r
I32 = mybir.dt.int32
U32 = mybir.dt.uint32

P = 128
D = 1024
T = 512
NT = T // P
KD = D // P
SG = 512
NF = SG // P
H = 8
HD = 64
C = P
LEVELS = 6
E = 32
TOPK = 4
NOVF = (T * TOPK) // (P + 1)
NB = E + NOVF
NT1 = NB + 1
FE = 2 * D
LIMIT = 7.0
ALPHA = 1.702
DECAY = float(np.exp(-0.5))
RMS_EPS = 1e-5
LN_EPS = 1e-5
LNX_EPS = 64e-5


def columns(*named):
    at, out = 0, {}
    for name, width in named:
        out[name] = slice(at, at + width)
        at += width
    return out, at


CST, NCST = columns(("ident", P), ("tri", 2 * C), ("mask", 4 * C), ("below", P), ("lev1", P),
                    ("ones", P), ("ident64", HD), ("head", NF * H), ("iota_e", E), ("iota_b", NT1),
                    ("iota_r", P), ("tok", NT), ("half", H * NT), ("over", E + 1), ("part", 1))
VEC, NVEC = columns(("norm1", KD), ("mu_rkv", 3 * NF), ("mu_wag", 3 * KD), ("a0", NF),
                    ("k_k", NF), ("k_a", NF), ("r_k", NF))


def constants():
    c = np.zeros((P, NCST), np.float32)
    s, t = np.arange(P)[:, None], np.arange(P)[None, :]
    c[:, CST["ident"]] = s == t
    mid = (s < C // 2).astype(np.float32)
    c[:, CST["tri"]] = -DECAY * np.concatenate([(s <= t) - mid, (s < t) - mid], 1)
    c[:, CST["mask"]] = np.concatenate([s < t, s <= t, s < t, s <= t], 1)
    c[:, CST["below"]] = s < t
    c[:, CST["lev1"]] = (s % 2 == 0) & (t == s + 1)
    c[:, CST["ones"]] = 1
    c[:, CST["ident64"]] = (s % HD) == np.arange(HD)[None, :]
    head = np.zeros((P, NF, H), np.float32)
    for f in range(NF):
        for q in range(2):
            head[HD * q:HD * q + HD, f, 2 * f + q] = 1
    c[:, CST["head"]] = head.reshape(P, -1)
    c[:, CST["iota_e"]] = np.arange(E)
    c[:, CST["iota_b"]] = np.arange(NT1)
    c[:, CST["iota_r"]] = np.arange(P)
    c[:, CST["tok"]] = np.arange(NT)[None, :] * P + s
    c[:, CST["half"]] = -0.5
    c[:E, CST["over"]] = np.concatenate([np.arange(E)[:, None] < np.arange(E)[None, :], np.ones((E, 1))], 1)
    c[:, CST["part"]] = s % E
    lev = np.zeros((P, LEVELS, HD), np.int32)
    for l in range(LEVELS):
        b = 2 << l
        col = np.arange(HD)
        lev[:, l, :] = (s // b) == (2 * (col // b) + 1)[None, :]
    return c, lev.reshape(P, -1)


class Chain:

    def __init__(self, eng, sem, base=0):
        self.eng, self.sem, self.base, self.n = eng, sem, base, 0

    def __call__(self, ins):
        ins.then_inc(self.sem, 1)
        self.n += 1
        self.eng.wait_ge(self.sem, self.base + self.n)


def program(nc, a):
    with ExitStack() as whole:
        sems = {}

        def sem(name):
            if name not in sems:
                sems[name] = whole.enter_context(nc.semaphore(name))
            return sems[name]

        def sb(stack, name, shape, dt=F32):
            return stack.enter_context(nc.sbuf_tensor(name, shape, dt))

        PS = whole.enter_context(nc.psum_tensor("PS", [P, 8, 512], F32))
        ring = sb(whole, "ring", [P, 12, FE])
        cst = sb(whole, "cst", [P, NCST])
        tok_of_row = sb(whole, "tok_of_row", [P, NT1], I32)
        slot_of = sb(whole, "slot_of", [P, NT * TOPK], I32)
        gate_of = sb(whole, "gate_of", [P, NT * TOPK])
        bias = sb(whole, "bias", [2 * E, FE + D], F32R)
        sel_of_block = sb(whole, "sel_of_block", [2 * E, NT1])
        expert_of_block = sb(whole, "expert_of_block", [1, NT1], I32)
        fresh_block = sb(whole, "fresh_block", [1, NT1], I32)
        n_blocks = sb(whole, "n_blocks", [1, 2], I32)
        ident = cst[:, CST["ident"]]

        xn_dram = nc.dram_tensor("xn_rows", [T, D], F32, kind="Internal").ap()
        h_dram = nc.dram_tensor("h_rows", [T, D], F32, kind="Internal").ap()
        y_dram = nc.dram_tensor("y_rows", [NB * P, D], F32, kind="Internal").ap()
        w1_rows = a["moe_w1"].rearrange("l e (k p) f -> l e k p f", p=P)
        w2_rows = a["moe_w2"].rearrange("l e (k p) f -> l e p k f", p=P)

        with ExitStack() as st:
            first_half(nc, st, a, sem, sb, PS, ring, cst, tok_of_row, slot_of, gate_of,
                       sel_of_block, expert_of_block, fresh_block, n_blocks, bias, xn_dram, h_dram, y_dram, w1_rows, w2_rows)
        with ExitStack() as st:
            experts(nc, st, a, sem, sb, PS, ring, cst, tok_of_row, slot_of, gate_of,
                    sel_of_block, expert_of_block, fresh_block, n_blocks, bias, xn_dram, h_dram, y_dram, w1_rows, w2_rows)


def first_half(nc, st, a, sem, sb, PS, ring, cst, tok_of_row, slot_of, gate_of,
               sel_of_block, expert_of_block, fresh_block, n_blocks, bias, xn_dram, h_dram, y_dram, w1_rows, w2_rows):
    ident = cst[:, CST["ident"]]
    ones = cst[:, CST["ones"]]
    vec = sb(st, "vec", [P, NVEC])

    def v(name, n=None, i=0):
        s = VEC[name]
        return vec[:, s] if n is None else vec[:, s.start + n * i:s.start + n * i + n]

    flat = ring[:, :, :].rearrange("p a b -> p (a b)")
    w_rkv = flat[:, 0:KD * 1536].rearrange("p (k n) -> p k n", k=KD)
    w_uv = flat[:, KD * 1536:KD * 2560].rearrange("p (k n) -> p k n", k=KD)
    w_out = flat[:, KD * 1536:KD * 1536 + KD * D].rearrange("p (k n) -> p k n", k=KD)
    lora_w = flat[:, 20480:22528].rearrange("p (k n) -> p k n", k=KD)
    lora_s = flat[:, 22528:24576].rearrange("p (k n) -> p k n", k=KD)

    def lent(at, *dims):
        n = int(np.prod(dims))
        names = "abcd"[:len(dims)]
        view = flat[:, at:at + n]
        if len(dims) > 1:
            view = view.rearrange(f"p ({' '.join(names)}) -> p {' '.join(names)}",
                                  **dict(zip(names, dims)))
        return view, at + n

    at = 0
    am, at = lent(at, H, 4 * C)
    sgt, at = lent(at, SG)
    ar, at = lent(at, NF, 2, C)
    loopb, at = lent(at, 12, SG)
    assert at <= KD * 1536
    at = KD * 1536
    wsT, at = lent(at, H, C)
    ln_rows, at = lent(at, 2, SG)
    bs, at = lent(at, NF * C)
    at = 20480
    uT, at = lent(at, NF, T)
    vN, at = lent(at, NF, SG)
    at = 20480
    anv, at = lent(at, H, 2 * HD)
    pq, at = lent(at, H, 2 * HD)
    tb, at = lent(at, H, C)
    ub, at = lent(at, H, C)
    assert at <= 24576

    x_t = sb(st, "x_t", [P, 2, D])
    hnT = sb(st, "hnT", [P, KD, T + 1])
    yT = hnT[:, :, 0:T]
    pT = [sb(st, f"p{n}T", [P, NF, T + 1]) for n in "rkv"]
    rT, kT, vT = pT
    dT = sb(st, "dT", [P, 2, T])
    icT = sb(st, "icT", [P, NF, T])
    kkT = sb(st, "kkT", [P, NF, T])
    sgN = sb(st, "sgN", [P, NT, SG])
    gateT = sb(st, "gateT", [P, T])
    tw_ = sb(st, "tw", [P, T])
    tw = tw_[0:HD + 1, :]
    ia = sb(st, "ia", [P, T])
    lora_w2_ = sb(st, "lora_w2", [P, SG])
    lora_w2 = lora_w2_[0:HD + 1, :]
    lora_a2 = sb(st, "lora_a2", [P, SG])
    lora_g2 = sb(st, "lora_g2", [P, SG])
    lev = sb(st, "lev", [P, LEVELS * HD], I32)
    small = sb(st, "small", [P, 160])
    headrk = sb(st, "headrk", [P, NF * H])
    rows = x_t[:, 1, :].rearrange("p (a b) -> p a b", a=2)
    (e_in, e_ex, e_inv, b_t, k_t, rk_t, bN, kN, vNt, z_b, gT, y_b) = (loopb[:, i, :] for i in range(12))
    sT = sb(st, "sT", [P, NF * HD])
    blank = sb(st, "blank", [P, P])
    s0, fT = lora_w2_[:, 0:NF * HD], lora_w2_[:, NF * HD:2 * NF * HD]
    gsl = tw_[:, 0:P]
    v_sl = lora_a2
    g_sb = ia
    y2 = dT[:, 0, :]
    y3 = dT[:, 1, :]
    ss = small[:, 0:NT]
    rstd = small[:, NT:2 * NT]
    bnst = small[:, 16:16 + 6]
    bnag = small[:, 24:24 + 2 * NT]
    vr = small[:, 32:32 + NT]
    omka = small[:, 40:40 + NF]
    kks = small[:, 48:48 + H * NT]
    kkr = small[:, 80:80 + H * NT]
    e_m = small[:, 112:112 + NF]
    mean = small[:, 120:128]
    var = small[:, 128:136]
    rs = small[:, 136:144]
    e_last = small[:, 152:152 + NF]

    x_rows = a["x"].rearrange("b (j p) d -> (b j) p d", p=P)
    w_in = a["w_in"].rearrange("l (k p) n -> (l p) k n", p=P)
    w_out_d = a["w_out"].rearrange("l (k p) n -> (l p) k n", p=P)
    N_ACT_USES = 30

    def hN(j):
        return kkT[:, :, :].rearrange("p a b -> p (a b)")[:, (j % 2) * D:(j % 2 + 1) * D] if j < 2 else \
            icT[:, :, :].rearrange("p a b -> p (a b)")[:, (j % 2) * D:(j % 2 + 1) * D]

    def xN(j):
        return sgN[:, :, :].rearrange("p a b -> p (a b)")[:, (j % 2) * D:(j % 2 + 1) * D] if j < 2 else \
            rT[:, :, :].rearrange("p a b -> p (a b)")[:, (j % 2) * D:(j % 2 + 1) * D]

    norm2 = kT[:, :, :].rearrange("p a b -> p (a b)")[:, 0:D]
    router_w = vT[:, :, :].rearrange("p a b -> p (a b)")[:, 0:KD * E].rearrange("p (k e) -> p k e", k=KD)
    router_b = vT[:, :, :].rearrange("p a b -> p (a b)")[:, 256:256 + E]
    bias_raw = flat[0:2 * E, 20480:20480 + FE + D]
    xnT = vT[:, :, :].rearrange("p a b -> p (a b)")[:, 512:512 + D].rearrange("p (k t) -> p k t", k=KD)
    route = hnT[:, :, :].rearrange("p a b -> p (a b)")
    roh = x_t[:, :, :].rearrange("p a b -> p (a b)").rearrange("p (i r) -> p i r", i=16)
    r_at = {}
    at = 0
    for name, n in (("logit", NT * E), ("top", NT * 8), ("idxf", NT * TOPK), ("oh", NT * TOPK * E),
                    ("m", NT * E), ("rank", NT * E), ("cntT", 8), ("ovfB", P), ("ovs", E + 1),
                    ("tmp", NT * TOPK * E), ("rk", 16), ("q", 16), ("q2", 16), ("blk", 16), ("ov", 16),
                    ("e0", 16), ("starts", E), ("et", NT1), ("fresh", NT1), ("boh", 16 * NT1), ("boh_tok", 16 * NT1), ("sm", 4), ("sr", 4)):
        r_at[name] = route[:, at:at + n]
        at += n
    assert at <= KD * (T + 1)
    idxu = gateT[:, 0:NT * 8].bitcast(U32)

    def y_half(q):
        return PS[:, 5, 0:NF * HD] if q == 0 else PS[:, 6, 0:NF * HD]

    AB_BANKS = (3, 7, 6, 5)

    def at(j, first=0):
        return bass.ds(j * C + first, C)

    def xs_view(j):
        return kkT[:, :, :].rearrange("p a b -> p (a b)")[:, (j % 2) * D:(j % 2 + 1) * D]

    def sq_view(n):
        return x_t[:, :, :].rearrange("p a b -> p (a b)")[:, n * SG:(n + 1) * SG]

    kkr_wide = sq_view

    r_at["begun"] = kT[:, :, :].rearrange("p a b -> p (a b)")[:, 0:NT1 * E]

    def xsq():
        return sgN[:, 0:2, :].rearrange("p a b -> p (a b)")

    block = st.enter_context(nc.Block())

    def f(n):
        return n.rearrange("p (f c) -> p f c", f=NF)

    @block.sync
    def _(sp):
        sp.dma_start(vec[:, :], a["vec"]).then_inc(sem("vec_in"), 16)
        for j in range(2):
            sp.dma_start(x_t[:, j, :], x_rows[j]).then_inc(sem(f"x_in{j}"), 16)
        sp.dma_start(cst[:, :], a["cst"]).then_inc(sem("cst_in"), 16)
        sp.dma_start(lora_w, a["lora_1"].rearrange("(k p) n -> p k n", p=P)).then_inc(sem("lora_in"), 16)
        sp.dma_start(lora_w2[:, :], a["lora_w2"]).then_inc(sem("lora2_in"), 16)
        sp.dma_start(lora_a2[HD:P, :], a["iclr_a2"][0]).then_inc(sem("lora2_in"), 16)
        sp.dma_start(lora_g2[:, :], a["gate_g2"][0]).then_inc(sem("lora2_in"), 16)
        for j in range(2, NT):
            sp.wait_ge(sem("xs_done"), j - 1)
            sp.dma_start(x_t[:, j % 2, :], x_rows[j]).then_inc(sem(f"x_in{j % 2}"), 16)
        for k in range(KD):
            sp.dma_start(w_uv[:, k, :], w_in[:, k, 0:2 * SG]).then_inc(sem("w_uv_in"), 16)
        for k in range(KD):
            sp.dma_start(w_rkv[:, k, :], w_in[:, k, 2 * SG:5 * SG]).then_inc(sem("w_rkv_in"), 16)
        sp.dma_start(lev[:, :], a["lev"]).then_inc(sem("lev_in"), 16)
        sp.wait_ge(sem("filled"), 10 + 2 * NF)
        sp.dma_start(wsT, a["sgu_wT"]).then_inc(sem("ws_in"), 16)
        for i, name in enumerate(("sgu_ln_g", "sgu_ln_b")):
            sp.dma_start(ln_rows[:, i, :], a[name].broadcast_to([P, SG])).then_inc(sem("rows_in"), 16)
        for q in range(2):
            src = a["sgu_b"][0].rearrange("(f q) i -> q f i", q=2)[q].rearrange("(o f) i -> o f i", o=1)
            sp.dma_start(f(bs)[HD * q:HD * q + HD], src.broadcast_to([HD, NF, C])).then_inc(sem("bs_in"), 16)
        sp.wait_ge(sem("sgu_out"), NF)
        sp.dma_start(w_out, w_out_d).then_inc(sem("w_out_in"), 16)
        sp.wait_ge(sem("zeros"), 7)
        for b in range(E, NB):
            sp.dma_start(y_dram[b * P:(b + 1) * P, :].rearrange("p (a c) -> p a c", c=P),
                         blank[:, :].rearrange("p (o c) -> p o c", o=1).broadcast_to([P, D // P, P])).then_inc(sem("rows_out"), 16)
        sp.wait_ge(sem("kk_turned"), NF)
        for i, name in enumerate(("lnx_g", "lnx_b")):
            sp.dma_start(rows[:, i, :], a[name].broadcast_to([P, SG])).then_inc(sem("lnx_in"), 16)
        sp.dma_start(x_t[:, 0, :], x_rows[0]).then_inc(sem("x_in0"), 16)
        sp.wait_ge(sem("y"), NT)
        for q in range(2):
            sp.dma_start(bias_raw[q * E:(q + 1) * E, 0:FE], a["moe_b1"][0]).then_inc(sem("bias_in"), 16)
            sp.dma_start(bias_raw[q * E:(q + 1) * E, FE:FE + D], a["moe_b2"][0]).then_inc(sem("bias_in"), 16)
        sp.wait_ge(sem("y_gated"), NT)
        sp.dma_start(x_t[:, 1, :], x_rows[1]).then_inc(sem("x_in1"), 16)
        sp.wait_ge(sem("y_out"), NT)
        for k in range(6):
            sp.dma_start(ring[:, k, :], w1_rows[0, 0, k]).then_inc(sem(f"w_in{k}"), 16)
        for j in range(2, NT):
            sp.wait_ge(sem("h_done"), j - 1)
            sp.dma_start(x_t[:, j % 2, :], x_rows[j]).then_inc(sem(f"x_in{j % 2}"), 16)
        sp.wait_ge(sem("out_proj"), NT)
        for k in range(6, KD):
            sp.dma_start(ring[:, k, :], w1_rows[0, 0, k]).then_inc(sem(f"w_in{k}"), 16)
        for c in range(KD, 12):
            if c == 10:
                sp.wait_ge(sem("bias_lo"), 1)
            k = 2 * (c - KD)
            sp.dma_start(ring[:, c, :].rearrange("p (k f) -> p k f", k=2), w2_rows[0, 0, :, k:k + 2, :]).then_inc(sem("w2_first"), 16)
        for j in range(NT):
            sp.wait_ge(sem("xn_done"), j + 1)
            sp.dma_start(h_dram[j * P:(j + 1) * P, :], hN(j)).then_inc(sem("rows_out"), 16)
            sp.dma_start(xn_dram[j * P:(j + 1) * P, :], xN(j)).then_inc(sem("rows_out"), 16)
        sp.wait_ge(sem("rows_out"), 16 * (2 * NT + NOVF))

    @block.gpsimd
    def _(pool):
        zeros = Chain(pool, sem("zeros"))
        zeros(nc.gpsimd.memset(hnT[:, :, 0:1], 0.0))
        for p_ in pT:
            zeros(nc.gpsimd.memset(p_[:, :, 0:1], 0.0))
        zeros(nc.gpsimd.memset(tw[HD:HD + 1, :], 1.0))
        zeros(nc.gpsimd.memset(sT[:, :], 0.0))
        zeros(nc.gpsimd.memset(blank[:, :], 0.0))
        pool.wait_ge(sem("cst_in"), 16)
        half = cst[:, CST["half"]]
        for j in range(NT):
            pool.wait_ge(sem("ms"), j + 1)
            nc.gpsimd.tensor_tensor(rstd[:, j:j + 1], ss[:, j:j + 1], half[:, 0:1], ALU.pow).then_inc(sem("rstd"), 1)
            pool.wait_ge(sem("rstd"), j + 1)
        pool.wait_ge(sem("ws_in"), 16)
        nc.gpsimd.memset(wsT[HD:P, :, 0:HD], 0.0).then_inc(sem("ws_masked"), 1)
        pool.wait_ge(sem("ws_masked"), 1)
        pool.wait_ge(sem("ln_var"), 1)
        nc.gpsimd.tensor_tensor(vr, vr, half[:, 0:NT], ALU.pow).then_inc(sem("ln_rs"), 1)
        pool.wait_ge(sem("ln_rs"), 1)
        pool.wait_ge(sem("kk_ss"), 1)
        nc.gpsimd.tensor_tensor(kkr, kks, half, ALU.pow).then_inc(sem("kk_rs"), 1)
        pool.wait_ge(sem("kk_rs"), 1)

        pool.wait_ge(sem("filled"), N_ACT_USES)
        pool.wait_ge(sem("sgu_out"), NF)
        nc.gpsimd.tensor_copy(yT[:, 0:NF, :], uT).then_inc(sem("sgu_moved"), 1)
        pool.wait_ge(sem("sgu_moved"), 1)

        def slices(before):
            j = before + 1
            pool.wait_ge(sem("cw"), j)
            pool.sem_inc(sem("wait_only_pool"), 1)
            nc.gpsimd.tensor_copy(sgt, sgN[:, bass.ds(j, 1), :].rearrange("p a b -> p (a b)")).then_inc(sem("sliced"), 1)
            pool.wait_ge(sem("sliced"), before * 3 + 1)
            pool.wait_ge(sem("v_turned"), j)
            pool.sem_inc(sem("wait_only_pool"), 1)
            nc.gpsimd.tensor_copy(f(v_sl[:, :]), vT[:, :, at(j, 1)]).then_inc(sem("sliced"), 1)
            pool.wait_ge(sem("sliced"), before * 3 + 2)
            pool.wait_ge(sem("gate"), j)
            pool.sem_inc(sem("wait_only_pool"), 1)
            nc.gpsimd.tensor_copy(gsl[:, :], gateT[:, at(j)]).then_inc(sem("sliced"), 1)
            pool.wait_ge(sem("sliced"), before * 3 + 3)

        def norm(j):
            hd = lambda t: t.rearrange("p (h d) -> p h d", h=H)
            wide = lambda t: t.rearrange("p (h o) -> p h o", o=1).broadcast_to([P, H, HD])
            step = Chain(pool, sem("pool_norm"), j * 5)
            pool.wait_ge(sem("bonus_read"), j + 2)
            step(nc.gpsimd.tensor_tensor(y3, y3, rows[:, 1, :], ALU.add))
            pool.wait_ge(sem("lnx_var"), j + 1)
            step(nc.gpsimd.tensor_tensor(rs, var, half[:, 0:H], ALU.pow))
            step(nc.gpsimd.tensor_tensor(hd(y_b), hd(y_b), wide(rs), ALU.mult))
            step(nc.gpsimd.tensor_tensor(y_b, y_b, rows[:, 0, :], ALU.mult))
            step(nc.gpsimd.tensor_tensor(y_b, y_b, y3, ALU.add))
            pool.wait_ge(sem("gate_out"), j + 1)
            nc.gpsimd.tensor_tensor(y_b, y_b, g_sb[:, :], ALU.mult).then_inc(sem("y_gated"), 1)
            pool.wait_ge(sem("y_gated"), j + 1)

        pool.wait_ge(sem("lnx_in"), 32)
        with pool.Fori(0, NT - 1) as j:
            slices(j)
            norm(j)
        norm(NT - 1)
        for j in range(NT):
            pool.wait_ge(sem("ms"), NT + j + 1)
            nc.gpsimd.tensor_tensor(rstd[:, j:j + 1], ss[:, j:j + 1], half[:, 0:1], ALU.pow).then_inc(sem("rstd"), 1)
            pool.wait_ge(sem("rstd"), NT + j + 1)

    @block.tensor
    def _(pe):
        pe.wait_ge(sem("cst_in"), 16)
        for j in range(NT):
            pe.wait_ge(sem("xs_done"), j + 1)
            for k in range(KD):
                m = nc.tensor.transpose(PS[:, 2 * j + k // 4, (k % 4) * P:(k % 4 + 1) * P], xs_view(j)[:, k * P:(k + 1) * P], ident)
            m.then_inc(sem("xT"), 1)
        pe.wait_ge(sem("hn_done"), 2 * NT)
        pe.wait_ge(sem("zeros"), 7)
        use = [0]

        def bank():
            u = use[0]
            use[0] += 1
            if u >= 6:
                pe.wait_ge(sem("emptied"), u - 5)
            return PS[:, u % 6, :]

        now, before = slice(1, T + 1), slice(0, T)
        pe.wait_ge(sem("lora_mixed"), 2)
        for m_ in range(2):
            out = bank()
            for k in range(KD):
                pe.matmul(out, lora_w[:, k, m_ * P:(m_ + 1) * P], hnT[:, k, now], start=(k == 0), stop=False)
                m = pe.matmul(out, lora_s[:, k, m_ * P:(m_ + 1) * P], hnT[:, k, before], start=False, stop=(k == KD - 1))
            m.then_inc(sem("filled"), 1)
        pe.wait_ge(sem("lora2_in"), 48)
        pe.wait_ge(sem("emptied"), 2)
        for n in range(NF):
            pe.matmul(bank(), lora_a2[HD:P, n * P:(n + 1) * P], ia[HD:P, :], start=True, stop=True).then_inc(sem("filled"), 1)
        for j in range(NT):
            pe.matmul(bank(), tw[:, j * P:(j + 1) * P], lora_w2[:, :], start=True, stop=True).then_inc(sem("filled"), 1)
        pe.wait_ge(sem("w_uv_in"), 16 * KD)
        for n in range(NF):
            out = bank()
            for k in range(KD):
                m = pe.matmul(out, w_uv[:, k, n * P:(n + 1) * P], hnT[:, k, now], start=(k == 0), stop=(k == KD - 1))
            m.then_inc(sem("filled"), 1)
        for j in range(NT):
            out = bank()
            for k in range(KD):
                m = pe.matmul(out, hnT[:, k, 1 + j * P:1 + (j + 1) * P], w_uv[:, k, SG:2 * SG],
                              start=(k == 0), stop=(k == KD - 1))
            m.then_inc(sem("filled"), 1)
        pe.wait_ge(sem("w_rkv_in"), 16 * KD)

        def log_decays(before=None):
            if before is None:
                pe.wait_ge(sem("emptied"), N_ACT_USES - 4)
                sg = sgN[:, 0, :]
            else:
                pe.wait_ge(sem("sliced"), before * 3 + 1)
                pe.wait_ge(sem("pq_out"), before * 2 + 2)
                sg = sgt
            for n in range(NF):
                m = pe.matmul(PS[:, n // 2, (n % 2) * 2 * C:(n % 2 + 1) * 2 * C], sg[:, n * P:(n + 1) * P],
                              cst[:, CST["tri"]], start=True, stop=True, skip_group_check=True)
            m.then_inc(sem("cw"), 1)

        def project(i, n):
            out = bank()
            for k in range(KD):
                m = pe.matmul(out, w_rkv[:, k, i * SG + n * P:i * SG + (n + 1) * P], hnT[:, k, now],
                              start=(k == 0), stop=(k == KD - 1))
            m.then_inc(sem("filled"), 1)

        for n in range(NF):
            project(1, n)
        pe.wait_ge(sem("ws_masked"), 1)
        pe.wait_ge(sem("ln_done"), NT)
        for n in range(NF):
            if n >= 1:
                pe.wait_ge(sem("mix_read"), n)
            for q in range(2):
                for j in range(NT):
                    h = 2 * n + q
                    m = pe.matmul(PS[HD * q:HD * q + HD, 7, j * P:(j + 1) * P], vN[:, j, h * HD:(h + 1) * HD],
                                  wsT[:, h, :], start=True, stop=True, skip_group_check=True)
            m.then_inc(sem("sgu_mixed"), 1)
            project(0, n)
        pe.wait_ge(sem("kk_sq"), NF)
        for j in range(NT):
            for n in range(NF):
                m = pe.matmul(PS[:, 6, j * H:(j + 1) * H], sq_view(n)[:, j * P:(j + 1) * P],
                              cst[:, CST["head"]][:, n * H:(n + 1) * H], start=(n == 0), stop=(n == NF - 1))
        m.then_inc(sem("kk_len"), 1)
        for n in range(NF):
            project(2, n)
            if n == NF - 1:
                log_decays()
            pe.wait_ge(sem("kk_wide"), n + 1)
            if n >= 1:
                pe.wait_ge(sem("kk_scaled"), n)
            for j in range(NT):
                m = nc.tensor.transpose(PS[:, 6, j * P:(j + 1) * P], kkr_wide(n)[:, j * P:(j + 1) * P], ident)
            m.then_inc(sem("kk_turned"), 1)
        assert use[0] == N_ACT_USES

        def level(j, l):
            b = 2 << l
            for g in range(2):
                pe.wait_ge(sem("t_done"), j * 2 * (LEVELS + 1) + 2 * l + g + 1)
                if l:
                    pe.wait_ge(sem("z_done"), j * 2 * LEVELS + 2 * l + g - 1)
                for h in range(4):
                    even = tb[:, 4 * g + h, :].rearrange("p (n t b) -> p n t b", t=2, b=b)[:, :, 0, :]
                    m = pe.matmul(PS[:, 2 + g, h * HD:(h + 1) * HD], am[:, 4 * g + h, 0:C], even,
                                  start=True, stop=True, skip_group_check=True)
                m.then_inc(sem("z"), 1)
            for g in range(2):
                pe.wait_ge(sem("z_done"), j * 2 * LEVELS + 2 * l + g + 1)
                if l:
                    pe.wait_ge(sem("u_done"), j * 2 * LEVELS + 2 * (l - 1) + g + 1)
                for h in range(4):
                    m = pe.matmul(PS[:, 2 + g, 256 + h * HD:256 + (h + 1) * HD], ub[:, 4 * g + h, :],
                                  z_b[:, g * 256 + h * HD:g * 256 + (h + 1) * HD], start=True, stop=True,
                                  skip_group_check=True)
                m.then_inc(sem("x"), 1)
            for g in range(2):
                pe.wait_ge(sem("t_done"), j * 2 * (LEVELS + 1) + 2 * (l + 1) + g + 1)
                for h in range(4):
                    m = nc.tensor.transpose(PS[:, 4 + g, h * P:(h + 1) * P], tb[:, 4 * g + h, :], ident)
                m.then_inc(sem("u"), 1)

        def products(j, before=None):
            def turn(src, b, done="turned"):
                for n in range(NF):
                    m = nc.tensor.transpose(PS[:, b, n * P:(n + 1) * P], src[:, n, :], ident)
                m.then_inc(sem(done), 1)

            if before is None:
                pe.wait_ge(sem("kk_scaled"), NF)
                pe.wait_ge(sem("emptied"), N_ACT_USES)
                turn(vT[:, :, 1:1 + C], 4, "v_turned")
            else:
                pe.wait_ge(sem("sliced"), before * 3 + 2)
                pe.wait_ge(sem("state_read"), j)
                turn(f(v_sl[:, :]), 4, "v_turned")
            pe.wait_ge(sem("prep"), j * 5 + 1)
            turn(ar[:, :, 0, :], 2)
            pe.wait_ge(sem("prep"), j * 5 + 3)
            pe.wait_ge(sem("exps"), j * 4 + 4)
            turn(f(b_t), 0)
            pe.wait_ge(sem("prep"), j * 5 + 4)
            turn(f(k_t), 1)
            for n in range(NF):
                if n == 0:
                    pe.wait_ge(sem("bonus_read"), j + 1)
                if n == 1:
                    pe.wait_ge(sem("y_read"), j + 1)
                if n >= 2:
                    pe.wait_ge(sem("am_done"), j * H + 2 * n - 2)
                b_first = f(b_t)
                for t, cols in ((b_first, slice(0, 2 * C)), (f(k_t), slice(2 * C, 4 * C))):
                    for q in range(2):
                        p0, b = HD * q, AB_BANKS[(2 * n + q) % 4]
                        m = pe.matmul(PS[:, b, cols], t[p0:p0 + HD, n, :],
                                      ar[p0:p0 + HD, n, :, :].rearrange("p a b -> p (a b)"),
                                      start=True, stop=True, skip_group_check=True)
                        if t is not b_first:
                            m.then_inc(sem("ab"), 1)

            def turn_inverse(g):
                pe.wait_ge(sem("u_init"), j * 2 + g + 1)
                for h in range(4):
                    m = nc.tensor.transpose(PS[:, 4 + g, h * P:(h + 1) * P], ub[:, 4 * g + h, :], ident)
                m.then_inc(sem("t_turned"), 1)

            pe.wait_ge(sem("turned_out"), j * 4 + 4)
            turn_inverse(0)
            pe.wait_ge(sem("prep"), j * 5 + 5)
            pe.wait_ge(sem("am_done"), j * H + 6)
            for n in range(NF):
                m = pe.matmul(PS[:, 7, 0:H], f(rk_t)[:, n, :], headrk[:, n * H:(n + 1) * H], start=(n == 0), stop=(n == NF - 1))
            m.then_inc(sem("bonus"), 1)
            if before is not None:
                pe.wait_ge(sem("sliced"), before * 3 + 3)
            pe.wait_ge(sem("am_done"), j * H + 7)
            pe.matmul(PS[:, 6, :], gateT[:, 0:C] if before is None else gsl[:, :], lora_g2[:, :],
                      start=True, stop=True).then_inc(sem("gate"), 1)
            pe.wait_ge(sem("am_done"), j * H + H)
            for h in range(H):
                m = pe.matmul(PS[:, 0, h * HD:(h + 1) * HD], am[:, h, 2 * C:3 * C], vNt[:, h * HD:(h + 1) * HD],
                              start=True, stop=True, skip_group_check=True)
            m.then_inc(sem("mv"), 1)
            turn_inverse(1)
            for l in range(2):
                level(j, l)

        def project_out(j):
            b = 2 * (j % 2)
            if j == 0:
                pe.wait_ge(sem("w_out_in"), 16)
                pe.wait_ge(sem("y_out"), NT - 1)
                pe.wait_ge(sem("pq_out"), 2 * NT)
            if j >= 2:
                pe.wait_ge(sem("h_done"), j - 1)
            if j == NT - 1:
                pe.wait_ge(sem("y_out"), NT)
            for n in range(2):
                for k in range(KD):
                    m = pe.matmul(PS[:, b + n, :], yT[:, k, j * P:(j + 1) * P], w_out[:, k, n * 512:(n + 1) * 512],
                                  start=(k == 0), stop=(k == KD - 1))
            m.then_inc(sem("out_proj"), 1)

        def outputs(j, last=False):
            for l in range(2, LEVELS):
                level(j, l)
            pe.wait_ge(sem("mv_out"), j + 1)
            for h in range(H):
                if h % 4 == 0:
                    pe.wait_ge(sem("u_done"), j * 2 * LEVELS + 2 * (LEVELS - 1) + h // 4 + 1)
                m = pe.matmul(PS[:, h // 4, (h % 4) * C:(h % 4 + 1) * C], ub[:, h, :], anv[:, h, :],
                              start=True, stop=True, skip_group_check=True)
                if h % 4 == 3:
                    m.then_inc(sem("pq"), 1)
            for n in range(NF):
                if n % 2 == 0:
                    pe.wait_ge(sem("pq_out"), j * 2 + n // 2 + 1)
                for bank_, width in ((2, C), (3, HD)):
                    for q in range(2):
                        p0, h = HD * q, 2 * n + q
                        rhs = am[:, h, C:2 * C] if bank_ == 2 else bN[:, h * HD:(h + 1) * HD]
                        m = pe.matmul(PS[p0:p0 + HD, bank_, n * width:(n + 1) * width], pq[:, h, 0:HD], rhs,
                                      start=True, stop=True, skip_group_check=True)
            m.then_inc(sem("gf"), 1)
            if not last:
                log_decays(j)
            else:
                project_out(0)
            pe.wait_ge(sem("gf_out"), j * 2 + 2)
            pe.wait_ge(sem("s0_ready"), j + 1)
            for n in range(NF if not last else 0):
                for part in range(3):
                    for q in range(2):
                        p0, h = HD * q, 2 * n + q
                        hv, nv = slice(h * HD, (h + 1) * HD), slice(n * HD, (n + 1) * HD)
                        lhs, rhs = ((bN[:, hv], pq[:, h, HD:2 * HD]), (kN[:, hv], vNt[:, hv]),
                                    (fT[p0:p0 + HD, nv], s0[p0:p0 + HD, nv]))[part]
                        m = pe.matmul(PS[p0:p0 + HD, 4, nv], lhs, rhs, start=(part == 0), stop=(part == 2), skip_group_check=True)
            if not last:
                m.then_inc(sem("state"), 1)
            pe.wait_ge(sem("gate_out"), j + 1)
            for h in range(H):
                n, p0, hv = h // 2, HD * (h % 2), slice(h * HD, (h + 1) * HD)
                yo = y_half(h % 2)[:, n * HD:(n + 1) * HD]
                pe.matmul(yo, am[:, h, C:2 * C], pq[:, h, HD:2 * HD], start=True, stop=False, skip_group_check=True)
                pe.matmul(yo, am[:, h, 3 * C:4 * C], vNt[:, hv], start=False, stop=False, skip_group_check=True)
                m = pe.matmul(yo, f(gT)[p0:p0 + HD, n, :], s0[p0:p0 + HD, n * HD:(n + 1) * HD],
                              start=False, stop=True, skip_group_check=True)
            m.then_inc(sem("y"), 1)

        def turn_y(j, bank=1):
            pe.wait_ge(sem("y_gated"), j + 1)
            for n in range(NF):
                m = nc.tensor.transpose(PS[:, bank, n * P:(n + 1) * P], y_b[:, n * P:(n + 1) * P], ident)
            m.then_inc(sem("y_turned"), 1)

        products(0)
        with pe.Fori(0, NT - 1) as j:
            outputs(j)
            products(j + 1, j)
            turn_y(j)
        outputs(NT - 1, last=True)

        def turn_xn(j):
            pe.wait_ge(sem("xn_done"), j + 1)
            if j:
                pe.wait_ge(sem("xnT_out"), j)
            for k in range(KD):
                m = nc.tensor.transpose(PS[:, 4 + k // 4, (k % 4) * P:(k % 4 + 1) * P], xN(j)[:, k * P:(k + 1) * P], ident)
            m.then_inc(sem("xn_turned"), 1)

        def logits(j):
            pe.wait_ge(sem("xnT_out"), j + 1)
            for k in range(KD):
                m = pe.matmul(PS[:, 7, j * E:(j + 1) * E], xnT[:, k, :], router_w[:, k, :],
                              start=(k == 0), stop=(k == KD - 1))
            m.then_inc(sem("logits"), 1)

        project_out(1)
        turn_y(NT - 1, bank=6)
        turn_xn(0)
        project_out(2)
        pe.wait_ge(sem("router_in"), 32)
        logits(0)
        turn_xn(1)
        project_out(3)
        logits(1)
        for j in range(2, NT):
            turn_xn(j)
            logits(j)
        pe.wait_ge(sem("mask_m"), 1)
        mm = r_at["m"].rearrange("p (j e) -> p j e", j=NT)
        for j in range(NT):
            for i in range(j):
                pe.matmul(PS[:, 0, j * E:(j + 1) * E], ones, mm[:, i, :], start=(i == 0), stop=False)
            pe.matmul(PS[:, 0, j * E:(j + 1) * E], cst[:, CST["below"]], mm[:, j, :], start=(j == 0), stop=True)
        for j in range(NT):
            m = pe.matmul(PS[0:E, 1, 0:1], mm[:, j, :], ones[:, 0:1], start=(j == 0), stop=(j == NT - 1))
        m.then_inc(sem("counts"), 1)
        pe.wait_ge(sem("ovf_b"), 1)
        pe.matmul(PS[:, 2, 0:E + 1], r_at["ovfB"][0:E, :], cst[0:E, CST["over"]], start=True, stop=True).then_inc(sem("ovf_sum"), 1)
        pe.wait_ge(sem("onehots"), 1)
        boh_tok = r_at["boh_tok"].rearrange("p (i b) -> p i b", i=16)
        for i in range(16):
            m = pe.matmul(PS[:, 3, 0:NT1], roh[:, i, :], boh_tok[:, i, :], start=(i == 0), stop=(i == 15))
        m.then_inc(sem("tok_table"), 1)
    @block.scalar
    def _(act):
        for j in range(NT):
            act.wait_ge(sem(f"x_in{j % 2}"), 16 * (j // 2 + 1))
            if j:
                act.wait_ge(sem("sumsq"), j)
            nc.scalar.activation(xsq(), x_t[:, j % 2, :], ACT.Square, accum_out=ss[:, j:j + 1]).then_inc(sem("sumsq"), 1)
        use = [0]

        def filled():
            act.wait_ge(sem("filled"), use[0] + 1)
            u = use[0]
            use[0] += 1
            return PS[:, u % 6, :]

        b = filled()
        nc.scalar.activation(tw[0:HD, :], b[0:HD, :], ACT.Tanh)
        nc.scalar.activation(ia[HD:P, :], b[HD:P, :], ACT.Copy).then_inc(sem("emptied"), 1)
        nc.scalar.activation(gateT[:, :], filled(), ACT.Sigmoid).then_inc(sem("emptied"), 1)
        for n in range(NF):
            nc.scalar.activation(icT[:, n, :], filled(), ACT.Sigmoid, bias=v("a0", 1, n)).then_inc(sem("emptied"), 1)
        for j in range(NT):
            nc.scalar.activation(sgN[:, j, :], filled(), ACT.Sigmoid).then_inc(sem("emptied"), 1)
        for n in range(NF):
            nc.scalar.activation(uT[:, n, :], filled(), ACT.Gelu).then_inc(sem("emptied"), 1)
        for j in range(NT):
            nc.scalar.activation(vN[:, j, :], filled(), ACT.Gelu).then_inc(sem("emptied"), 1)
        for i in (1, 0, 2):
            for n in range(NF):
                nc.scalar.activation(pT[i][:, n, 1:T + 1], filled(), ACT.Copy).then_inc(sem("emptied"), 1)
        def exps(j, first=False):
            if not first:
                act.wait_ge(sem("prep"), j * 5)
                act.wait_ge(sem("s0_ready"), j)
            act.wait_ge(sem("cw"), j + 1)
            cw = PS[:, 0:2, :].rearrange("p a b -> p (a b)").rearrange("p (f c) -> p f c", f=NF)
            nc.scalar.activation(f(e_ex), cw[:, :, C:2 * C], ACT.Exp).then_inc(sem("exps"), 1)
            nc.scalar.activation(f(e_in), cw[:, :, 0:C], ACT.Exp).then_inc(sem("exps"), 1)
            nc.scalar.activation(f(e_inv), cw[:, :, 0:C], ACT.Exp, scale=-1.0).then_inc(sem("exps"), 1)
            nc.scalar.activation(e_m.rearrange("p (f o) -> p f o", o=1), cw[:, :, C:C + 1], ACT.Exp, scale=-1.0).then_inc(sem("exps"), 1)

        def level(j, l):
            for g in range(2):
                act.wait_ge(sem("z"), j * 2 * LEVELS + 2 * l + g + 1)
                nc.scalar.activation(z_b[:, g * 256:(g + 1) * 256], PS[:, 2 + g, 0:256], ACT.Copy).then_inc(sem("z_done"), 1)
            for g in range(2):
                act.wait_ge(sem("u"), j * 2 * LEVELS + 2 * l + g + 1)
                nc.scalar.activation(ub[:, 4 * g:4 * g + 4, :].rearrange("p h t -> p (h t)"), PS[:, 4 + g, :], ACT.Copy).then_inc(sem("u_done"), 1)

        def products(j):
            act.wait_ge(sem("v_turned"), j + 1)
            act.wait_ge(sem("bonus_read"), j + 1)
            nc.scalar.activation(vNt, PS[:, 4, :], ACT.Copy).then_inc(sem("turned_out"), 1)
            for i, (dst, b) in enumerate(((anv[:, :, 0:HD], 2), (bN, 0), (kN, 1))):
                act.wait_ge(sem("turned"), j * 3 + i + 1)
                src = PS[:, b, :]
                if i == 0:
                    src = src.rearrange("p (h d) -> p h d", h=H)
                nc.scalar.activation(dst, src, ACT.Copy).then_inc(sem("turned_out"), 1)
            act.wait_ge(sem("mv"), j + 1)
            nc.scalar.activation(anv[:, :, HD:2 * HD], PS[:, 0, :].rearrange("p (h d) -> p h d", h=H), ACT.Copy).then_inc(sem("mv_out"), 1)
            for l in range(2):
                level(j, l)

        def outputs(j, last=False):
            for l in range(2, LEVELS):
                level(j, l)
                if l == 3:
                    act.wait_ge(sem("gate"), j + 1)
                    nc.scalar.activation(g_sb[:, :], PS[:, 6, :], ACT.Copy).then_inc(sem("gate_out"), 1)
            for i in range(2):
                act.wait_ge(sem("pq"), j * 2 + i + 1)
                nc.scalar.activation(pq[:, 4 * i:4 * i + 4, :].rearrange("p h t -> p (h t)"), PS[:, i, :], ACT.Copy).then_inc(sem("pq_out"), 1)
            if not last:
                exps(j + 1)
            act.wait_ge(sem("y_read"), j + 2)
            nc.scalar.activation(y2, y_b, ACT.Square).then_inc(sem("y_squared"), 1)

        def y_out(j, bank=1):
            act.wait_ge(sem("y_turned"), j + 1)
            nc.scalar.activation(yT[:, NF:2 * NF, at(j)], f(PS[:, bank, :]), ACT.Copy).then_inc(sem("y_out"), 1)

        exps(0, first=True)
        act.wait_ge(sem("sgu_moved"), 1)
        products(0)
        with act.Fori(0, NT - 1) as j:
            outputs(j)
            products(j + 1)
            y_out(j)
        outputs(NT - 1, last=True)
        act.wait_ge(sem("prep"), 5 * NT)
        act.wait_ge(sem("sliced"), 3 * (NT - 1))
        act.dma_start(norm2, a["norm2_g"].broadcast_to([P, D])).then_inc(sem("norm2_in"), 16)
        act.dma_start(router_w, a["router_w"].rearrange("l (k p) e -> (l p) k e", p=P)).then_inc(sem("router_in"), 16)
        act.dma_start(router_b, a["router_b"].broadcast_to([P, E])).then_inc(sem("router_in"), 16)
        act.wait_ge(sem("bias_one"), 1)
        nc.scalar.activation(bias[:, :], bias_raw, ACT.Copy).then_inc(sem("bias_hi"), 1)
        for j in range(NT):
            act.wait_ge(sem("h_done"), j + 1)
            nc.scalar.activation(xN(j), hN(j), ACT.Square, accum_out=ss[:, j:j + 1]).then_inc(sem("sumsq"), 1)
            if j == 0:
                y_out(NT - 1, bank=6)
        act.wait_ge(sem("gate_in"), 1)
        top = r_at["top"].rearrange("p (j t) -> p j t", j=NT)
        nc.scalar.activation(gate_of[:, :].rearrange("p (j k) -> p j k", j=NT), top[:, :, 0:TOPK], ACT.Exp).then_inc(sem("gate_exp"), 1)

    @block.vector
    def _(dve):
        step = Chain(dve, sem("dve_step"))
        dve.wait_ge(sem("cst_in"), 16)
        dve.wait_ge(sem("vec_in"), 16)

        def scale(j):
            dve.wait_ge(sem("rstd"), j + 1)
            if j >= 2:
                dve.wait_ge(sem("xT"), j - 1)
            nc.vector.tensor_scalar(xs_view(j), x_t[:, j % 2, :], rstd[:, j:j + 1], None, ALU.mult).then_inc(sem("xs_done"), 1)

        def evac(j):
            dve.wait_ge(sem("xT"), j + 1)
            for q in range(2):
                g = v("norm1")[:, 4 * q:4 * q + 4].rearrange("p (k o) -> p k o", o=1).broadcast_to([P, 4, P])
                nc.vector.tensor_tensor(hnT[:, 4 * q:4 * q + 4, 1 + j * P:1 + (j + 1) * P],
                                        PS[:, 2 * j + q, :].rearrange("p (k t) -> p k t", k=4), g, ALU.mult).then_inc(sem("hn_done"), 1)

        def mix_lora():
            dve.wait_ge(sem("lora_in"), 16)
            mw = v("mu_wag").rearrange("p (i k o) -> p i k o", i=3, o=1)
            for i, (lo, n) in enumerate(((0, HD), (HD, HD), (P, P))):
                step(nc.vector.tensor_tensor(lora_s[:, :, lo:lo + n], lora_w[:, :, lo:lo + n],
                                             mw[:, i].broadcast_to([P, KD, n]), ALU.mult))
            nc.vector.tensor_tensor(lora_w, lora_w, lora_s, ALU.subtract).then_inc(sem("lora_mixed"), 2)

        for j in range(NT):
            dve.wait_ge(sem("sumsq"), j + 1)
            nc.vector.tensor_scalar(ss[:, j:j + 1], ss[:, j:j + 1], 1.0 / D, RMS_EPS, ALU.mult, ALU.add).then_inc(sem("ms"), 1)
            scale(j)
            if j == 1:
                mix_lora()
            if j:
                evac(j - 1)
        evac(NT - 1)
        step(nc.vector.tensor_scalar(omka, v("k_a"), -1.0, 1.0, ALU.mult, ALU.add))
        for n in range(NF):
            step(nc.vector.tensor_scalar(headrk[:, n * H:(n + 1) * H], cst[:, CST["head"]][:, n * H:(n + 1) * H],
                                         v("r_k", 1, n), None, ALU.mult))

        def mix(i, n, at):
            dve.wait_ge(sem("emptied"), at + n + 1)
            step(nc.vector.tensor_tensor(dT[:, 0, :], pT[i][:, n, 0:T], pT[i][:, n, 1:T + 1], ALU.subtract))
            step(nc.vector.scalar_tensor_tensor(pT[i][:, n, 1:T + 1], dT[:, 0, :], v("mu_rkv", NF, i)[:, n:n + 1],
                                                pT[i][:, n, 1:T + 1], ALU.mult, ALU.add))

        dve.wait_ge(sem("rows_in"), 32)
        for j in range(NT):
            dve.wait_ge(sem("emptied"), 10 + NF + j + 1)
            step(nc.vector.bn_stats(bnst, vN[:, j, :]))
            step(nc.vector.bn_aggr(bnag[:, 2 * j:2 * j + 2], bnst))
        nc.vector.tensor_scalar(vr, bnag.rearrange("p (j t) -> p j t", t=2)[:, :, 1], LN_EPS, None, ALU.add).then_inc(sem("ln_var"), 1)
        dve.wait_ge(sem("ln_rs"), 1)
        for j in range(NT):
            step(nc.vector.tensor_scalar(vN[:, j, :], vN[:, j, :], bnag[:, 2 * j:2 * j + 1], vr[:, j:j + 1], ALU.subtract, ALU.mult))
            step(nc.vector.tensor_tensor(vN[:, j, :], vN[:, j, :], ln_rows[:, 0, :], ALU.mult))
            nc.vector.tensor_tensor(vN[:, j, :], vN[:, j, :], ln_rows[:, 1, :], ALU.add).then_inc(sem("ln_done"), 1)
        dve.wait_ge(sem("zeros"), 7)
        for n in range(NF):
            mix(1, n, 18)
            step(nc.vector.tensor_scalar(kkT[:, n, :], kT[:, n, 1:T + 1], v("k_k", 1, n), None, ALU.mult))
            nc.vector.tensor_tensor(sq_view(n), kkT[:, n, :], kkT[:, n, :], ALU.mult).then_inc(sem("kk_sq"), 1)
            step(nc.vector.tensor_scalar(dT[:, 1, :], icT[:, n, :], v("k_a", 1, n), omka[:, n:n + 1], ALU.mult, ALU.add))
            step(nc.vector.tensor_tensor(kT[:, n, 1:T + 1], kT[:, n, 1:T + 1], dT[:, 1, :], ALU.mult))
        dve.wait_ge(sem("bs_in"), 32)
        for n in range(NF):
            dve.wait_ge(sem("sgu_mixed"), n + 1)
            b4 = f(bs)[:, n:n + 1, :].broadcast_to([P, NT, C])
            nc.vector.tensor_tensor(dT[:, 0, :].rearrange("p (j i) -> p j i", j=NT),
                                    PS[:, 7, :].rearrange("p (j i) -> p j i", j=NT), b4, ALU.add).then_inc(sem("mix_read"), 1)
            dve.wait_ge(sem("mix_read"), n + 1)
            nc.vector.tensor_tensor(uT[:, n, :], dT[:, 0, :], uT[:, n, :], ALU.mult).then_inc(sem("sgu_out"), 1)
            dve.wait_ge(sem("sgu_out"), n + 1)
            mix(0, n, 22)
        dve.wait_ge(sem("kk_len"), 1)
        nc.vector.tensor_scalar(kks, PS[:, 6, 0:H * NT], 1e-24, None, ALU.max).then_inc(sem("kk_ss"), 1)
        dve.wait_ge(sem("kk_rs"), 1)
        kkr4 = kkr.rearrange("p (j f q o) -> p j f q o", j=NT, f=NF, q=2)
        for n in range(NF):
            nc.vector.tensor_copy(kkr_wide(n).rearrange("p (j q c) -> p j q c", j=NT, q=2),
                                  kkr4[:, :, n].broadcast_to([P, NT, 2, HD])).then_inc(sem("kk_wide"), 1)
        for n in range(NF):
            mix(2, n, 26)
            dve.wait_ge(sem("kk_turned"), n + 1)
            nc.vector.tensor_tensor(kkT[:, n, :], kkT[:, n, :], PS[:, 6, :], ALU.mult).then_inc(sem("kk_scaled"), 1)
        dve.wait_ge(sem("lev_in"), 16)
        before = step.n
        for free in ("bonus_read", "y_read"):
            dve.sem_inc(sem(free), 1)

        hd = lambda t: t.rearrange("p (h d) -> p h d", h=H)
        wide = lambda t: t.rearrange("p (h o) -> p h o", o=1)
        halves = lambda t, n: t.rearrange("p (n q d) -> p q n d", q=2, d=n)
        col = lambda t: t.rearrange("p (f o) -> p f o", o=1)

        def prepare(j):
            step = Chain(dve, sem("dve_prep"), j)
            dve.wait_ge(sem("exps"), j * 4 + 1)
            nc.vector.scalar_tensor_tensor(ar[:, :, 0, :], kkT[:, :, at(j)], -1.0, f(e_ex), ALU.mult, ALU.mult).then_inc(sem("prep"), 1)
            dve.wait_ge(sem("exps"), j * 4 + 2)
            nc.vector.tensor_tensor(ar[:, :, 1, :], rT[:, :, at(j, 1)], f(e_in), ALU.mult).then_inc(sem("prep"), 1)
            step(nc.vector.tensor_tensor(f(b_t), kkT[:, :, at(j)], icT[:, :, at(j)], ALU.mult))
            dve.wait_ge(sem("exps"), j * 4 + 3)
            nc.vector.tensor_tensor(b_t, b_t, e_inv, ALU.mult).then_inc(sem("prep"), 1)
            nc.vector.tensor_tensor(f(k_t), kT[:, :, at(j, 1)], f(e_inv), ALU.mult).then_inc(sem("prep"), 1)
            nc.vector.tensor_tensor(f(rk_t), rT[:, :, at(j, 1)], kT[:, :, at(j, 1)], ALU.mult).then_inc(sem("prep"), 1)

        def start_state(j):
            dve.wait_ge(sem("exps"), j * 4 + 4)
            nc.vector.tensor_copy(col(e_last), f(e_in)[:, :, C - 1:C]).then_inc(sem("e_last"), 1)
            dve.wait_ge(sem("e_last"), j + 1)
            nc.vector.tensor_tensor(f(s0[:, :]), f(sT[:, :]), col(e_m).broadcast_to([P, NF, HD]), ALU.mult).then_inc(sem("s0_ready"), 1)

        def grow(j, l):
            b = 2 << l
            for g in range(2):
                dve.wait_ge(sem("x"), j * 2 * LEVELS + 2 * l + g + 1)
                dve.sem_inc(sem("wait_only"), 1)
                even = tb[:, 4 * g:4 * g + 4, :].rearrange("p h (n t b) -> p h n t b", t=2, b=b)[:, :, :, 0, :]
                mask = lev[:, l * HD:(l + 1) * HD].rearrange("p (o n b) -> p o n b", o=1, b=b).broadcast_to([P, 4, HD // b, b])
                xv = PS[:, 2 + g, 256:512].rearrange("p (h n b) -> p h n b", h=4, b=b)
                nc.vector.copy_predicated(even, mask, xv).then_inc(sem("t_done"), 1)

        def products(j):
            step = Chain(dve, sem("dve_inverse"), j * 2)
            for h in range(H):
                dve.wait_ge(sem("ab"), j * H + h + 1)
                nc.vector.tensor_tensor(am[:, h, :], PS[:, AB_BANKS[h % 4], :], cst[:, CST["mask"]], ALU.mult).then_inc(sem("am_done"), 1)
                if h % 4 == 3:
                    g = h // 4
                    dve.wait_ge(sem("am_done"), j * H + h + 1)
                    u4 = ub[:, 4 * g:4 * g + 4, :]
                    l1 = cst[:, CST["lev1"]].rearrange("p (o t) -> p o t", o=1).broadcast_to([P, 4, C])
                    i1 = ident.rearrange("p (o t) -> p o t", o=1).broadcast_to([P, 4, C])
                    step(nc.vector.tensor_tensor(u4, am[:, 4 * g:4 * g + 4, 0:C], l1, ALU.mult))
                    nc.vector.tensor_tensor(u4, u4, i1, ALU.add).then_inc(sem("u_init"), 1)
            for g in range(2):
                dve.wait_ge(sem("t_turned"), j * 2 + g + 1)
                nc.vector.tensor_copy(tb[:, 4 * g:4 * g + 4, :].rearrange("p h t -> p (h t)"), PS[:, 4 + g, :]).then_inc(sem("t_done"), 1)
            for l in range(2):
                grow(j, l)

        OUT_STEPS = 5

        def outputs(j, last=False):
            step = Chain(dve, sem("dve_out"), j * OUT_STEPS)
            for l in range(2, LEVELS):
                grow(j, l)
            dve.wait_ge(sem("gf"), j + 1)
            i64 = cst[:, CST["ident64"]].rearrange("p (o t) -> p o t", o=1).broadcast_to([P, NF, HD])
            nc.vector.tensor_tensor(f(fT[:, :]), f(PS[:, 3, 0:NF * HD]), i64, ALU.add).then_inc(sem("gf_out"), 1)
            nc.vector.tensor_tensor(f(gT), f(PS[:, 2, :]), ar[:, :, 1, :], ALU.add).then_inc(sem("gf_out"), 1)
            dve.wait_ge(sem("bonus"), j + 1)
            nc.vector.tensor_tensor(hd(y3), hd(vNt), wide(PS[:, 7, 0:H]).broadcast_to([P, H, HD]), ALU.mult).then_inc(sem("bonus_read"), 1)
            if not last:
                dve.wait_ge(sem("gf_out"), j * 2 + 2)
                prepare(j + 1)
            if not last:
                dve.wait_ge(sem("state"), j + 1)
                nc.vector.tensor_tensor(f(sT[:, :]), f(PS[:, 4, 0:NF * HD]), col(e_last).broadcast_to([P, NF, HD]), ALU.mult).then_inc(sem("state_read"), 1)
            dve.wait_ge(sem("y"), j + 1)
            for q in range(2):
                step(nc.vector.tensor_reduce(halves(mean, 1)[:, q], y_half(q).rearrange("p (n d) -> p n d", n=NF), AX_X, ALU.add))
            step(nc.vector.tensor_scalar(mean, mean, 1.0 / HD, None, ALU.mult))
            for q in range(2):
                ins = nc.vector.tensor_tensor(halves(y_b, HD)[:, q], y_half(q).rearrange("p (n d) -> p n d", n=NF),
                                              halves(mean, 1)[:, q].broadcast_to([P, NF, HD]), ALU.subtract)
                step(ins) if q == 0 else ins.then_inc(sem("y_read"), 1)
            if not last:
                dve.wait_ge(sem("state_read"), j + 1)
                start_state(j + 1)
            dve.wait_ge(sem("y_squared"), j + 1)
            step(nc.vector.tensor_reduce(var, hd(y2), AX_X, ALU.add))
            nc.vector.tensor_scalar(var, var, 1.0 / HD, LNX_EPS, ALU.mult, ALU.add).then_inc(sem("lnx_var"), 1)
            assert step.n == OUT_STEPS, step.n

        dve.wait_ge(sem("kk_scaled"), NF)
        prepare(0)
        start_state(0)
        dve.wait_ge(sem("sgu_moved"), 1)
        products(0)
        with dve.Fori(0, NT - 1) as j:
            outputs(j)
            products(j + 1)
        outputs(NT - 1, last=True)

        step = Chain(dve, sem("dve_step"), before)

        def norm2_rows(j):
            b = 2 * (j % 2)
            dve.wait_ge(sem("out_proj"), j + 1)
            dve.wait_ge(sem(f"x_in{j % 2}"), 16 * (j // 2 + 1 + 2))
            nc.vector.tensor_tensor(hN(j), PS[:, b:b + 2, :].rearrange("p a b -> p (a b)"), x_t[:, j % 2, :], ALU.add).then_inc(sem("h_done"), 1)
            dve.wait_ge(sem("sumsq"), NT + j + 1)
            nc.vector.tensor_scalar(ss[:, j:j + 1], ss[:, j:j + 1], 1.0 / D, RMS_EPS, ALU.mult, ALU.add).then_inc(sem("ms"), 1)
            dve.wait_ge(sem("rstd"), NT + j + 1)
            nc.vector.scalar_tensor_tensor(xN(j), hN(j), rstd[:, j:j + 1], norm2, ALU.mult, ALU.mult).then_inc(sem("xn_done"), 1)

        def xn_out(j):
            dve.wait_ge(sem("xn_turned"), j + 1)
            if j:
                dve.wait_ge(sem("logits"), j)
            nc.vector.tensor_copy(xnT.rearrange("p k t -> p (k t)"), PS[:, 4:6, :].rearrange("p a b -> p (a b)")).then_inc(sem("xnT_out"), 1)

        linear = bias_raw[:, 0:FE].rearrange("p (f t) -> p f t", t=2)[:, :, 1]
        dve.wait_ge(sem("bias_in"), 64)
        nc.vector.tensor_scalar(linear, linear, 1.0, None, ALU.add).then_inc(sem("bias_one"), 1)
        dve.wait_ge(sem("prep"), 5 * NT)
        dve.wait_ge(sem("sliced"), 3 * (NT - 1))
        dve.wait_ge(sem("norm2_in"), 16)
        norm2_rows(0)
        dve.wait_ge(sem("bias_hi"), 1)
        low_half = slice(E, 2 * E)
        dve.wait_ge(sem("bias_one"), 1)
        nc.vector.tensor_tensor(bias[low_half, :], bias_raw[low_half, :], bias[low_half, :].bitcast(F32), ALU.subtract).then_inc(sem("bias_lo"), 1)
        norm2_rows(1)
        xn_out(0)
        norm2_rows(2)
        xn_out(1)
        norm2_rows(3)
        xn_out(2)
        xn_out(3)
        jk = lambda t, n: t.rearrange("p (j e) -> p j e", j=NT)
        logit, top, idxf = jk(r_at["logit"], E), jk(r_at["top"], 8), r_at["idxf"]
        dve.wait_ge(sem("logits"), NT)
        dve.wait_ge(sem("router_in"), 32)
        step(nc.vector.tensor_tensor(logit, jk(PS[:, 7, 0:NT * E], E),
                                     router_b.rearrange("p (o e) -> p o e", o=1).broadcast_to([P, NT, E]), ALU.add))
        for j in range(NT):
            step(nc.vector.max(top[:, j, :], logit[:, j, :]))
            step(nc.vector.max_index(jk(idxu, 8)[:, j, :], top[:, j, :], logit[:, j, :]))
        step(nc.vector.tensor_copy(jk(idxf, TOPK), jk(idxu, 8)[:, :, 0:TOPK]))
        t4 = r_at["e0"]
        step(nc.vector.tensor_copy(t4[:, 0:NT].rearrange("p (j o) -> p j o", o=1), top[:, :, 0:1]))
        nc.vector.tensor_tensor(top[:, :, 0:TOPK], top[:, :, 0:TOPK],
                                t4[:, 0:NT].rearrange("p (j o) -> p j o", o=1).broadcast_to([P, NT, TOPK]), ALU.subtract).then_inc(sem("gate_in"), 1)
        oh = r_at["oh"].rearrange("p (i e) -> p i e", e=E)
        iota_e = cst[:, CST["iota_e"]].rearrange("p (o e) -> p o e", o=1).broadcast_to([P, 16, E])
        step(nc.vector.tensor_tensor(oh, idxf.rearrange("p (i o) -> p i o", o=1).broadcast_to([P, 16, E]), iota_e, ALU.is_equal))
        oh4 = r_at["oh"].rearrange("p (j k e) -> p j k e", j=NT, k=TOPK)
        m = jk(r_at["m"], E)
        step(nc.vector.tensor_tensor(m, oh4[:, :, 0], oh4[:, :, 1], ALU.add))
        step(nc.vector.tensor_tensor(m, m, oh4[:, :, 2], ALU.add))
        nc.vector.tensor_tensor(m, m, oh4[:, :, 3], ALU.add).then_inc(sem("mask_m"), 1)
        g16 = gate_of[:, :].rearrange("p (j k) -> p j k", j=NT)
        dve.wait_ge(sem("gate_exp"), 1)
        step(nc.vector.tensor_reduce(r_at["sm"], g16, AX_X, ALU.add))
        step(nc.vector.reciprocal(r_at["sr"], r_at["sm"]))
        step(nc.vector.tensor_tensor(g16, g16, r_at["sr"].rearrange("p (j o) -> p j o", o=1).broadcast_to([P, NT, TOPK]), ALU.mult))
        dve.wait_ge(sem("counts"), 1)
        cn = r_at["cntT"][0:E, :]
        step(nc.vector.tensor_copy(cn[:, 0:1], PS[0:E, 1, 0:1]))
        step(nc.vector.tensor_scalar(cn[:, 1:2], cn[:, 0:1], float(P), None, ALU.is_gt))
        for i in (2, 3):
            step(nc.vector.scalar_tensor_tensor(cn[:, i:i + 1], cn[:, 0:1], float(i * P), cn[:, i - 1:i], ALU.is_gt, ALU.add))
        nc.vector.tensor_scalar(r_at["ovfB"][0:E, :], ones[0:E, :], cn[:, 3:4], None, ALU.mult).then_inc(sem("ovf_b"), 1)
        rank = jk(r_at["rank"], E)
        step(nc.vector.tensor_copy(rank, jk(PS[:, 0, 0:NT * E], E)))
        tmp = r_at["tmp"].rearrange("p (j k e) -> p j k e", j=NT, k=TOPK)
        for kk_ in range(TOPK):
            step(nc.vector.tensor_tensor(tmp[:, :, kk_], oh4[:, :, kk_], rank, ALU.mult))
        rk, q, q2, blk, ov = (r_at[n] for n in ("rk", "q", "q2", "blk", "ov"))
        tmp16 = r_at["tmp"].rearrange("p (i e) -> p i e", e=E)
        step(nc.vector.tensor_reduce(rk, tmp16, AX_X, ALU.add))
        dve.wait_ge(sem("ovf_sum"), 1)
        ovs = r_at["ovs"]
        step(nc.vector.tensor_copy(ovs, PS[:, 2, 0:E + 1]))
        step(nc.vector.tensor_tensor(tmp16, oh, ovs[:, 0:E].rearrange("p (o e) -> p o e", o=1).broadcast_to([P, 16, E]), ALU.mult))
        step(nc.vector.tensor_reduce(ov, tmp16, AX_X, ALU.add))
        step(nc.vector.tensor_scalar(q, rk, float(P), None, ALU.is_ge))
        for i in (2, 3):
            step(nc.vector.scalar_tensor_tensor(q, rk, float(i * P), q, ALU.is_ge, ALU.add))
        step(nc.vector.scalar_tensor_tensor(rk, q, -float(P), rk, ALU.mult, ALU.add))
        step(nc.vector.tensor_tensor(blk, ov, q, ALU.add))
        step(nc.vector.tensor_tensor(blk, blk, idxf, ALU.add))
        step(nc.vector.scalar_tensor_tensor(ov, blk, float(P), rk, ALU.mult, ALU.add))
        step(nc.vector.tensor_copy(slot_of[:, :], ov))
        boh = r_at["boh"].rearrange("p (i b) -> p i b", i=16)
        step(nc.vector.tensor_tensor(boh, blk.rearrange("p (i o) -> p i o", o=1).broadcast_to([P, 16, NT1]),
                                     cst[:, CST["iota_b"]].rearrange("p (o b) -> p o b", o=1).broadcast_to([P, 16, NT1]), ALU.is_equal))
        step(nc.vector.tensor_tensor(roh, rk.rearrange("p (i o) -> p i o", o=1).broadcast_to([P, 16, P]),
                                     cst[:, CST["iota_r"]].rearrange("p (o r) -> p o r", o=1).broadcast_to([P, 16, P]), ALU.is_equal))
        boh_tok = r_at["boh_tok"].rearrange("p (j k b) -> p j (k b)", j=NT, k=TOPK)
        step(nc.vector.tensor_tensor(boh_tok, r_at["boh"].rearrange("p (j c) -> p j c", j=NT),
                                     cst[:, CST["tok"]].rearrange("p (j o) -> p j o", o=1).broadcast_to([P, NT, TOPK * NT1]), ALU.mult))
        dve.sem_inc(sem("onehots"), 1)
        starts, et, fresh = r_at["starts"], r_at["et"], r_at["fresh"]
        begun = r_at["begun"].rearrange("p (b e) -> p b e", e=E)
        iota_b = cst[:, CST["iota_b"]]
        step(nc.vector.tensor_tensor(starts, ovs[:, 0:E], cst[:, CST["iota_e"]], ALU.add))
        step(nc.vector.tensor_tensor(begun, iota_b.rearrange("p (b o) -> p b o", o=1).broadcast_to([P, NT1, E]),
                                     starts.rearrange("p (o e) -> p o e", o=1).broadcast_to([P, NT1, E]), ALU.is_ge))
        step(nc.vector.tensor_reduce(et, begun, AX_X, ALU.add))
        step(nc.vector.tensor_scalar(et, et, -1.0, None, ALU.add))
        step(nc.vector.tensor_copy(expert_of_block[:, :], et[0:1, :]))
        step(nc.vector.tensor_scalar(sel_of_block[:, :], et[0:2 * E, :], cst[0:2 * E, CST["part"]], None, ALU.is_equal))
        step(nc.vector.tensor_tensor(fresh[:, 0:1], et[:, 0:1], et[:, 0:1], ALU.not_equal))
        step(nc.vector.tensor_tensor(fresh[:, 1:NT1], et[:, 1:NT1], et[:, 0:NT1 - 1], ALU.not_equal))
        step(nc.vector.tensor_copy(fresh_block[:, :], fresh[0:1, :]))
        nb = small[0:1, 0:2]
        step(nc.vector.tensor_scalar(nb[:, 0:1], ovs[0:1, E:E + 1], float(E - 1), None, ALU.add))
        step(nc.vector.tensor_scalar(nb[:, 1:2], ovs[0:1, E:E + 1], float(E - 2), None, ALU.add))
        step(nc.vector.tensor_copy(n_blocks[:, :], nb))
        dve.wait_ge(sem("tok_table"), 1)
        step(nc.vector.tensor_copy(tok_of_row[:, :], PS[:, 3, 0:NT1]))


def experts(nc, st, a, sem, sb, PS, ring, cst, tok_of_row, slot_of, gate_of,
            sel_of_block, expert_of_block, fresh_block, n_blocks, bias, xn_dram, h_dram, y_dram, w1_rows, w2_rows):
    ident = cst[:, CST["ident"]]
    HL = 3
    CH = 12
    w_hi = sb(st, "w_hi", [P, HL, FE], F32R)
    w_lo = sb(st, "w_lo", [P, HL, FE], F32R)
    x_hi = sb(st, "x_hi", [P, D], F32R)
    x_lo = sb(st, "x_lo", [P, D], F32R)
    a_hi = sb(st, "a_hi", [P, D], F32R)
    a_lo = sb(st, "a_lo", [P, D], F32R)
    pick_up = sb(st, "pick_up", [2 * E, P], F32R)
    pick_down = sb(st, "pick_down", [2 * E, P], F32R)
    x_rows = sb(st, "x_rows", [P, D])
    glu = sb(st, "glu", [P, D])
    sig = sb(st, "sig", [P, D])
    hid = sb(st, "hid", [P, D])
    y_out = sb(st, "y_out", [P, D])
    index = sb(st, "index", [P, 1], I32)
    stat = sb(st, "stat", [P, 16])
    flat = ring[:, :, :].rearrange("p a b -> p (a b)")
    h_rows = [flat[:, j * D:(j + 1) * D] for j in range(NT)]
    final_g = flat[:, NT * D:(NT + 1) * D]
    hidP = PS[:, 0:4, :].rearrange("p a b -> p (a b)")
    turnP = PS[:, 4:6, :].rearrange("p a b -> p (a b)")
    outP = PS[:, 6:8, :].rearrange("p a b -> p (a b)")
    picked_rows = [flat[:, (6 + q) * D:(7 + q) * D] for q in range(4)] + [t[:, :] for t in (x_rows, glu, sig, hid)]

    def one(i):
        return slice(i, i + 1) if isinstance(i, int) else bass.ds(i, 1)

    block = st.enter_context(nc.Block())

    def load_count(eng, less=0):
        return eng.value_load(n_blocks[0:1, less:less + 1], min_val=E - 1 - less, max_val=NB - 1 - less)

    @block.sync
    def _(sp):
        n1 = load_count(sp)
        sp.wait_ge(sem("w2_first"), 64)

        def expert(i):
            return sp.value_load(expert_of_block[0:1, one(i)], min_val=0, max_val=E - 1)

        def fresh(i):
            return sp.value_load(fresh_block[0:1, one(i)], min_val=0, max_val=1)

        def load_w1(i, before):
            e = expert(i)
            with sp.If(fresh(i) != 0):
                for c in range(KD):
                    sp.wait_ge(sem("split"), before * CH + c + 1)
                    sp.dma_start(ring[:, c, :], w1_rows[0, one(e), c].rearrange("o p f -> (o p) f")).then_inc(sem(f"w_in{c}"), 16)
            with sp.Else():
                for c in range(KD):
                    sp.wait_ge(sem("split"), before * CH + c + 1)
                    sp.sem_inc(sem(f"w_in{c}"), 16)

        def load_w2(i, before):
            e = expert(i)
            with sp.If(fresh(i) != 0):
                for c in range(KD, CH):
                    sp.wait_ge(sem("split"), before * CH + c + 1)
                    k = 2 * (c - KD)
                    sp.dma_start(ring[:, c, :].rearrange("p (k f) -> p k f", k=2),
                                 w2_rows[0, one(e), :, k:k + 2, :].rearrange("o p k f -> (o p) k f")).then_inc(sem(f"w_in{c}"), 16)
            with sp.Else():
                for c in range(KD, CH):
                    sp.wait_ge(sem("split"), before * CH + c + 1)
                    sp.sem_inc(sem(f"w_in{c}"), 16)

        with sp.Fori(0, n1) as i0:
            load_w1(i0 + 1, i0)
            load_w2(i0, i0)
        load_w2(n1, n1)
        sp.wait_ge(sem("split"), n1 * CH + KD)
        for j in range(NT):
            sp.dma_start(h_rows[j], h_dram[j * P:(j + 1) * P, :]).then_inc(sem("h_in"), 16)
        sp.dma_start(final_g, a["final_g"].rearrange("(o d) -> o d", o=1).broadcast_to([P, D])).then_inc(sem("h_in"), 16)
        for j in range(NT):
            sp.wait_ge(sem("out_done"), j + 1)
            sp.dma_start(a["out"][0, j * P:(j + 1) * P, :], h_rows[j]).then_inc(sem("out_stored"), 16)
        sp.wait_ge(sem("out_stored"), 16 * NT)

    @block.gpsimd
    def _(pool):
        n1, n2 = load_count(pool), load_count(pool, 1)
        pool.sem_inc(sem("y_free"), 1)

        def gather(i):
            pool.sem_inc(sem("wait_only_pool"), 1)
            nc.gpsimd.tensor_copy(index[:, :], tok_of_row[:, one(i)]).then_inc(sem("index"), 1)
            pool.wait_ge(sem("index"), i + 1)
            pool.sem_inc(sem("wait_only_pool"), 1)
            nc.gpsimd.indirect_dma_start(x_rows[:, :], None, xn_dram,
                                         bass.IndirectOffsetOnAxis(index[:, :], 0)).then_inc(sem("x_rows_in"), 16)

        def gate(i):
            pool.wait_ge(sem("hid_read"), i + 1)
            nc.gpsimd.tensor_tensor(hid[:, :], hid[:, :], glu[:, :], ALU.mult).then_inc(sem("scaled"), 1)
            pool.wait_ge(sem("scaled"), i + 1)
            pool.wait_ge(sem("sig"), i + 1)
            nc.gpsimd.tensor_tensor(hid[:, :], hid[:, :], sig[:, :], ALU.mult).then_inc(sem("hid_done"), 1)
            pool.wait_ge(sem("hid_done"), i + 1)

        def store(i):
            pool.wait_ge(sem("y_ready"), i + 2)
            pool.dma_start(y_dram[bass.ds(i * P, P), :], y_out[:, :]).then_inc(sem("y_stored"), 16)
            pool.wait_ge(sem("y_stored"), (i + 1) * 16)
            pool.sem_inc(sem("y_free"), 1)

        gather(0)
        pool.wait_ge(sem("x_turned"), 1)
        gather(1)
        pool.wait_ge(sem("x_turned"), 2)
        gather(2)
        gate(0)
        with pool.Fori(0, n2) as i1:
            i = i1 + 2
            pool.wait_ge(sem("x_turned"), i + 1)
            gather(i + 1)
            gate(i1 + 1)
            store(i1)
        gate(n1)
        store(n2)
        store(n1)
        def last_scale(j):
            pool.wait_ge(sem("final_ms"), j + 1)
            nc.gpsimd.tensor_tensor(stat[:, 8 + j:9 + j], stat[:, j:j + 1], cst[:, CST["half"]][:, 0:1], ALU.pow).then_inc(sem("final_rs"), 1)
            pool.wait_ge(sem("final_rs"), j + 1)

        for q in range(NT * TOPK):
            if q == 12:
                last_scale(0)
            place = q % len(picked_rows)
            if q >= len(picked_rows):
                pool.wait_ge(sem("summed"), q - len(picked_rows) + 1)
            nc.gpsimd.indirect_dma_start(picked_rows[place], None, y_dram,
                                         bass.IndirectOffsetOnAxis(slot_of[:, q:q + 1], 0)).then_inc(sem(f"row_in{place}"), 16)
        for j in range(1, NT):
            last_scale(j)

    @block.tensor
    def _(pe):
        n1 = load_count(pe)

        def turn(src, done):
            for k in range(KD):
                m = nc.tensor.transpose(turnP[:, k * P:(k + 1) * P], src[:, k * P:(k + 1) * P], ident)
            m.then_inc(sem(done), 1)

        def turn_x(i):
            pe.wait_ge(sem("x_rows_in"), (i + 1) * 16)
            turn(x_rows, "x_turned")

        def turn_a(i):
            pe.wait_ge(sem("hid_done"), i + 1)
            pe.wait_ge(sem("x_split"), i + 2)
            turn(hid, "a_turned")

        def bias_rows(out, pick, lo, n_):
            for q in range(n_):
                pe.matmul(out[:, q * 512:(q + 1) * 512], pick[:, :], bias[:, lo + q * 512:lo + (q + 1) * 512],
                          start=True, stop=False, skip_group_check=True)

        def products(out, hi, lo, wh, wl, n_, stop):
            for x, w in ((hi, wh), (hi, wl), (lo, wh)):
                for q in range(n_):
                    m = pe.matmul(out[:, q * 512:(q + 1) * 512], x, w[:, q * 512:(q + 1) * 512], start=False,
                                  stop=stop and x is lo, skip_group_check=True)
            return m

        def up(i):
            first = isinstance(i, int)
            pe.wait_ge(sem("x_split"), i + 1)
            if not first:
                pe.wait_ge(sem("hid_read"), i)
            bias_rows(hidP, pick_up, 0, 4)
            for c in range(KD):
                pe.wait_ge(sem("split"), i * CH + c + 1)
                s = c % HL
                k = slice(c * P, (c + 1) * P)
                m = products(hidP, x_hi[:, k], x_lo[:, k], w_hi[:, s, :], w_lo[:, s, :], 4, c == KD - 1)
                m.then_inc(sem("used"), 5 if first and c == KD - 1 else 1)
                if c == 3 and not first:
                    turn_a(i0)

        def down(i, last=False):
            pe.wait_ge(sem("a_split"), i + 1)
            pe.wait_ge(sem("y_ready"), i + 1)
            bias_rows(outP, pick_down, FE, 2)
            for c in range(KD, CH):
                pe.wait_ge(sem("split"), (i + 1) * CH + (c - KD if last else c) + 1)
                s = (c - KD if last else c) % HL
                for kk in range(2):
                    k = 2 * (c - KD) + kk
                    ks, fs = slice(k * P, (k + 1) * P), slice(kk * D, (kk + 1) * D)
                    m = products(outP, a_hi[:, ks], a_lo[:, ks], w_hi[:, s, fs], w_lo[:, s, fs], 2, k == KD - 1)
                m.then_inc(sem("used"), 1)

        turn_x(0)
        up(0)
        turn_x(1)
        with pe.Fori(0, n1) as i0:
            i = i0 + 1
            up(i)
            pe.wait_ge(sem("a_split"), i)
            turn_x(i + 1)
            down(i0)
        turn_a(n1)
        down(n1, last=True)

    @block.scalar
    def _(act):
        n1, n2 = load_count(act), load_count(act, 1)
        act.sem_inc(sem("y_ready"), 1)

        def high(c, i, last=False):
            cc = c - KD if last else c
            if not (isinstance(i, int) and i == 0 and c < HL):
                act.wait_ge(sem("used"), i * CH + (cc - HL + 1))
            act.wait_ge(sem(f"w_in{c}"), (i + 1) * 16 if c < KD else i * 16)
            first_end = isinstance(i, int) and i == 0 and c == KD - 1
            nc.scalar.activation(w_hi[:, cc % HL, :], ring[:, c, :], ACT.Copy).then_inc(sem("high"), 5 if first_end else 1)

        def x_high(i):
            act.wait_ge(sem("x_turned"), i + 1)
            nc.scalar.activation(x_hi[:, :], turnP, ACT.Copy).then_inc(sem("x_high"), 1)

        def a_high(i):
            act.wait_ge(sem("a_turned"), i + 1)
            nc.scalar.activation(a_hi[:, :], turnP, ACT.Copy).then_inc(sem("a_high"), 1)

        def sigmoid(i):
            act.wait_ge(sem("glu"), i + 1)
            nc.scalar.activation(sig[:, :], glu[:, :], ACT.Sigmoid, scale=ALPHA).then_inc(sem("sig"), 1)

        def out_rows(i, used):
            act.wait_ge(sem("used"), used)
            act.wait_ge(sem("y_free"), i + 1)
            nc.scalar.activation(y_out[:, :], outP, ACT.Copy).then_inc(sem("y_ready"), 1)

        x_high(0)
        for c in range(KD):
            high(c, 0)
        x_high(1)

        def step(i, i_1):
            high(0, i)
            sigmoid(i_1)
            high(1, i)
            if not isinstance(i, int):
                out_rows(i1, i1 * CH + 2 * CH)
            for c in range(2, 7):
                high(c, i)
            a_high(i_1)
            for c in range(7, 11):
                high(c, i)
            x_high(i + 1)
            high(11, i)

        step(1, 0)
        with act.Fori(0, n2) as i1:
            step(i1 + 2, i1 + 1)
        sigmoid(n1)
        out_rows(n2, n2 * CH + 2 * CH)
        a_high(n1)
        for c in range(KD, CH):
            high(c, n1 + 1, last=True)
        out_rows(n1, n1 * CH + CH + 4)
        for j in range(NT):
            act.wait_ge(sem("summed"), TOPK * (j + 1))
            if j:
                act.wait_ge(sem("final_sq"), j)
            nc.scalar.activation(y_out[:, :], h_rows[j], ACT.Square, accum_out=stat[:, j:j + 1]).then_inc(sem("final_sq"), 1)

    @block.vector
    def _(dve):
        n1 = load_count(dve)
        ones = cst[0:2 * E, CST["ones"]]

        def pick(dst, i):
            nc.vector.tensor_scalar(dst[:, :], ones, sel_of_block[:, one(i)], None, ALU.mult)

        def low(c, i, last=False):
            cc = c - KD if last else c
            dve.wait_ge(sem("high"), i * CH + cc + 1)
            s = cc % HL
            first_end = isinstance(i, int) and c == KD - 1
            nc.vector.tensor_tensor(w_lo[:, s, :], ring[:, c, :], w_hi[:, s, :].bitcast(F32), ALU.subtract) \
                .then_inc(sem("split"), 5 if first_end else 1)

        def x_low(i):
            dve.wait_ge(sem("x_high"), i + 1)
            pick(pick_up, i)
            nc.vector.tensor_tensor(x_lo[:, :], turnP, x_hi[:, :].bitcast(F32), ALU.subtract).then_inc(sem("x_split"), 1)

        def a_low(i):
            dve.wait_ge(sem("a_high"), i + 1)
            pick(pick_down, i)
            nc.vector.tensor_tensor(a_lo[:, :], turnP, a_hi[:, :].bitcast(F32), ALU.subtract).then_inc(sem("a_split"), 1)

        pairs = hidP.rearrange("p (f t) -> p f t", t=2)

        def clamp(i):
            dve.wait_ge(sem("used"), i * CH + KD)
            nc.vector.tensor_scalar(glu[:, :], pairs[:, :, 0], LIMIT, None, ALU.min).then_inc(sem("glu"), 1)
            nc.vector.tensor_scalar(hid[:, :], pairs[:, :, 1], LIMIT + 1, 1 - LIMIT, ALU.min, ALU.max).then_inc(sem("hid_read"), 1)

        x_low(0)
        for c in range(KD):
            low(c, 0)
        x_low(1)
        clamp(0)
        with dve.Fori(0, n1) as i0:
            i = i0 + 1
            for c in range(7):
                low(c, i)
            a_low(i0)
            for c in range(7, 11):
                low(c, i)
            x_low(i + 1)
            low(11, i)
            clamp(i)
        a_low(n1)
        for c in range(KD, CH):
            low(c, n1 + 1, last=True)
        dve.wait_ge(sem("h_in"), 16 * (NT + 1))
        def last_norm(j):
            dve.wait_ge(sem("final_sq"), j + 1)
            nc.vector.tensor_scalar(stat[:, j:j + 1], stat[:, j:j + 1], 1.0 / D, RMS_EPS, ALU.mult, ALU.add).then_inc(sem("final_ms"), 1)
            dve.wait_ge(sem("final_rs"), j + 1)
            nc.vector.scalar_tensor_tensor(h_rows[j], h_rows[j], stat[:, 8 + j:9 + j], final_g, ALU.mult, ALU.mult).then_inc(sem("out_done"), 1)

        for j in range(NT):
            for k in range(TOPK):
                q = j * TOPK + k
                place = q % len(picked_rows)
                dve.wait_ge(sem(f"row_in{place}"), 16 * (q // len(picked_rows) + 1))
                if k:
                    dve.wait_ge(sem("summed"), q)
                nc.vector.scalar_tensor_tensor(h_rows[j], picked_rows[place], gate_of[:, q:q + 1], h_rows[j],
                                               ALU.mult, ALU.add).then_inc(sem("summed"), 1)
                if k == 2 and j:
                    last_norm(j - 1)
        last_norm(NT - 1)


def features(x):
    return np.ascontiguousarray(x.reshape(-1, P).T)


def kernel(**inputs):
    import concourse.bacc as bacc
    from concourse.bass_utils import run_bass_kernel_spmd

    i = {k: np.asarray(v) for k, v in inputs.items()}
    cst, lev = constants()
    arrays = {n: i[n] for n in ("x", "w_in", "sgu_ln_g", "sgu_ln_b", "sgu_b", "iclr_a2", "gate_g2", "lnx_g", "lnx_b",
                                "w_out", "norm2_g", "router_w", "router_b", "moe_w1", "moe_b1", "moe_w2", "moe_b2",
                                "final_g")}
    arrays["cst"], arrays["lev"] = cst, lev
    arrays["vec"] = np.concatenate([features(i["norm1_g"][0])] + [features(i["mu_rkv"][0, q]) for q in range(3)]
                                   + [features(i["mu_wag"][0, q]) for q in range(3)]
                                   + [features(i[n][0]) for n in ("iclr_a0", "k_k", "k_a", "r_k")], 1)
    arrays["lora_1"] = np.concatenate([i["decay_w1"][0], i["iclr_a1"][0], i["gate_g1"][0]], 1)
    arrays["lora_w2"] = np.concatenate([i["decay_w2"][0], i["decay_w0"]], 0)
    arrays["sgu_wT"] = np.ascontiguousarray(i["sgu_w"][0].transpose(2, 0, 1))
    nc = bacc.Bacc("TRN2", target_bir_lowering=False, num_devices=1)
    a = {n: nc.dram_tensor("in_" + n, v.shape, mybir.dt.from_np(v.dtype), kind="ExternalInput").ap() for n, v in arrays.items()}
    a["out"] = nc.dram_tensor("out_rows", [1, T, D], F32, kind="ExternalOutput").ap()
    program(nc, a)
    r = run_bass_kernel_spmd(nc, [{"in_" + n: v for n, v in arrays.items()}], core_ids=[0])
    return r.results[0]["out_rows"]
```
